# Optimizing a Trainium2 kernel written in Bass

```python
import jax, jax.numpy as jnp
from jax import lax
import numpy as np

D_MODEL = 1024
BATCH = 1
SEQ = 128
DEPTH = 1
DEC_BATCH = 1
DEC_SEQ = 256
PAST_LEN = 128

GRID_W = 64
NORM_EPS = 1e-6
HEAD_R = 64
D_R = D_MODEL // 2
H_R = D_R // HEAD_R
DECAY_RANK = 64
AAA_RANK = 64
GATE_RANK = 128
GN_EPS = 64e-5
HEAD_DIM = 64
N_HEADS = (D_MODEL // 2) // HEAD_DIM
N_KV = N_HEADS // 4
GROUP = N_HEADS // N_KV
D_A = N_HEADS * HEAD_DIM
AXIS_DIM = HEAD_DIM // 2
ROPE_THETA = 10000.0
Q_BLOCK = 128
N_EXPERTS = 32
TOP_K = 4
D_FF = D_MODEL
SWIGLU_ALPHA = 1.702
SWIGLU_LIMIT = 7.0
MOE_BLOCK = 128
IN_SIZES = (D_R, D_R, D_R, DECAY_RANK, DECAY_RANK, AAA_RANK, AAA_RANK, GATE_RANK,
            D_A, N_KV * HEAD_DIM, N_KV * HEAD_DIM, D_MODEL, D_MODEL)
IN_COLS = sum(IN_SIZES)

kernel_name = "hybrid_rwkv7_gqa_moe_diffusion_step"

def rmsnorm(x, g):
    xf = x.astype(jnp.float32)
    y = xf * lax.rsqrt(jnp.mean(xf * xf, axis=-1, keepdims=True) + NORM_EPS)
    return (y * g.astype(jnp.float32)).astype(x.dtype)

def adaln(cond, w_ada, b_ada):
    mod = jax.nn.silu(cond) @ w_ada + b_ada
    return jnp.split(mod[:, None, :], 6, axis=-1)

def rope_2d(x):
    T = x.shape[1]
    rows = T // GRID_W
    row = jnp.repeat(jnp.arange(rows, dtype=jnp.float32), GRID_W)
    col = jnp.tile(jnp.arange(GRID_W, dtype=jnp.float32), rows)
    inv = ROPE_THETA ** (-jnp.arange(0, AXIS_DIM, 2, dtype=jnp.float32) / AXIS_DIM)

    def rot(xa, pos):
        ang = pos[:, None] * inv[None, :]
        cos = jnp.cos(ang)[None, :, None, :]
        sin = jnp.sin(ang)[None, :, None, :]
        x1, x2 = jnp.split(xa, 2, axis=-1)
        return jnp.concatenate([x1 * cos - x2 * sin, x2 * cos + x1 * sin], axis=-1)

    xr, xc = jnp.split(x.astype(jnp.float32), 2, axis=-1)
    return jnp.concatenate([rot(xr, row), rot(xc, col)], axis=-1).astype(x.dtype)

def block_attention(q, k, v):
    B, Sq, _, Dh = q.shape
    nb = Sq // Q_BLOCK
    scale = Dh ** -0.5
    qb = q.reshape(B, nb, Q_BLOCK, N_KV, GROUP, Dh).transpose(1, 0, 2, 3, 4, 5)

    def one_block(qblk):
        s = jnp.einsum("bqkgd,bskd->bkgqs", qblk, k).astype(jnp.float32) * scale
        p = jax.nn.softmax(s, axis=-1).astype(v.dtype)
        return jnp.einsum("bkgqs,bskd->bqkgd", p, v)

    o = lax.map(one_block, qb)
    return o.transpose(1, 0, 2, 3, 4, 5).reshape(B, Sq, N_HEADS * Dh)

def rwkv_scan(r, w, k, v, kk, a, s0, reverse):
    def step(S, xs):
        r_t, w_t, k_t, v_t, kk_t, a_t = xs
        sa = jnp.einsum("bhvk,bhk->bhv", S, kk_t)
        S = (S * w_t[:, :, None, :] - sa[..., None] * (kk_t * a_t)[:, :, None, :]
             + v_t[..., None] * k_t[:, :, None, :])
        return S, jnp.einsum("bhvk,bhk->bhv", S, r_t)

    xs = tuple(jnp.swapaxes(t, 0, 1) for t in (r, w, k, v, kk, a))
    s_fin, ys = lax.scan(step, s0.astype(jnp.float32), xs, reverse=reverse)
    return jnp.swapaxes(ys, 0, 1), s_fin

def rwkv7_bidir(r, k, v, wd, ad, gd, s0, lp):
    B, T, _ = r.shape

    def heads(t):
        return t.astype(jnp.float32).reshape(B, T, H_R, HEAD_R)

    rf, kf, vf = heads(r), heads(k), heads(v)
    kk = heads(k * lp["rw_kk"])
    kk = kk * lax.rsqrt(jnp.sum(kk * kk, axis=-1, keepdims=True) + 1e-12)
    k_a = lp["rw_ka"].astype(jnp.float32).reshape(H_R, HEAD_R)
    r_k = lp["rw_rk"].astype(jnp.float32)
    ys, bonus, finals = [], [], []
    for d in range(2):
        w_log = -jax.nn.softplus(-(lp["rw_w0"][d] + jnp.tanh(wd[d]) @ lp["rw_w2"][d])) - 0.5
        decay = jnp.exp(-jnp.exp(heads(w_log)))
        a = jax.nn.sigmoid(heads(lp["rw_a0"][d] + ad[d] @ lp["rw_a2"][d]))
        kd = kf * (1.0 + (a - 1.0) * k_a)
        y, s_fin = rwkv_scan(rf, decay, kd, vf, kk, a, s0[d], reverse=(d == 1))
        ys.append(y)
        bonus.append(jnp.sum(rf * kd * r_k, axis=-1, keepdims=True) * vf)
        finals.append(s_fin)
    y = ys[0] + ys[1]
    mu = jnp.mean(y, axis=-1, keepdims=True)
    var = jnp.mean(jnp.square(y - mu), axis=-1, keepdims=True)
    yn = ((y - mu) * lax.rsqrt(var + GN_EPS)).reshape(B, T, D_R)
    yn = yn * lp["rw_ln_w"] + lp["rw_ln_b"] + (bonus[0] + bonus[1]).reshape(B, T, D_R)
    g = jax.nn.sigmoid(gd) @ lp["rw_g2"]
    return (yn * g).astype(r.dtype), finals[0], finals[1]

def token_mixer(h, lp, s0_f, s0_b, ctx_k, ctx_v):
    B, T, _ = h.shape
    z = h @ lp["w_in"]
    offs = np.cumsum(IN_SIZES)[:-1].tolist()
    (r, k, v, wd_f, wd_b, ad_f, ad_b, gd, q, ka, va, gate_r, gate_a) = jnp.split(z, offs, axis=-1)
    y_r, s_f, s_b = rwkv7_bidir(r, k, v, (wd_f, wd_b), (ad_f, ad_b), gd, (s0_f, s0_b), lp)
    qh = rmsnorm(q.reshape(B, T, N_HEADS, HEAD_DIM), lp["q_norm"])
    kh = rmsnorm(ka.reshape(B, T, N_KV, HEAD_DIM), lp["k_norm"])
    vh = va.reshape(B, T, N_KV, HEAD_DIM)
    if ctx_k is None:
        y_a = block_attention(qh, kh, vh)
    else:
        k_all = jnp.concatenate([rope_2d(kh), ctx_k.astype(kh.dtype)], axis=1)
        v_all = jnp.concatenate([vh, ctx_v.astype(vh.dtype)], axis=1)
        y_a = block_attention(rope_2d(qh), k_all, v_all)
    merged = (jax.nn.sigmoid(gate_r) * (y_r @ lp["w_up_r"])
              + jax.nn.sigmoid(gate_a) * (y_a @ lp["w_up_a"]))
    return merged @ lp["w_out"], kh, vh, s_f, s_b

def routed_ffn(h, lp):
    n, d_model = h.shape
    nk = n * TOP_K
    logits = (h @ lp["w_router"] + lp["b_router"]).astype(jnp.float32)
    top_val, top_idx = lax.top_k(logits, TOP_K)
    gates = jax.nn.softmax(top_val, axis=-1)
    flat_e = top_idx.reshape(nk).astype(jnp.int32)
    flat_t = jnp.arange(nk, dtype=jnp.int32) // TOP_K
    flat_g = gates.reshape(nk)
    order = jnp.argsort(flat_e)
    e_s, t_s, g_s = flat_e[order], flat_t[order], flat_g[order]
    counts = jnp.bincount(flat_e, length=N_EXPERTS)
    start = jnp.cumsum(counts) - counts
    padded = (counts + MOE_BLOCK - 1) // MOE_BLOCK * MOE_BLOCK
    pstart = jnp.cumsum(padded) - padded
    dest = pstart[e_s] + jnp.arange(nk, dtype=jnp.int32) - start[e_s]
    n_blocks = -(-nk // MOE_BLOCK) + N_EXPERTS
    cap = n_blocks * MOE_BLOCK
    slot_t = jnp.zeros((cap,), jnp.int32).at[dest].set(t_s)
    slot_g = jnp.zeros((cap,), jnp.float32).at[dest].set(g_s)
    slot_e = jnp.full((cap,), N_EXPERTS - 1, jnp.int32).at[dest].set(e_s)
    block_e = slot_e[::MOE_BLOCK]
    xs = h[slot_t].reshape(n_blocks, MOE_BLOCK, d_model)
    w1, b1, w2, b2 = lp["w_moe_in"], lp["b_moe_in"], lp["w_moe_out"], lp["b_moe_out"]

    def run_block(args):
        xb, e = args
        hb = xb @ w1[e] + b1[e]
        glu, lin = jnp.split(hb, 2, axis=-1)
        glu = jnp.minimum(glu, SWIGLU_LIMIT)
        lin = jnp.clip(lin, -SWIGLU_LIMIT, SWIGLU_LIMIT)
        act = glu * jax.nn.sigmoid(SWIGLU_ALPHA * glu) * (lin + 1.0)
        return act @ w2[e] + b2[e]

    ys = lax.map(run_block, (xs, block_e)).reshape(cap, d_model)
    return jnp.zeros_like(h).at[slot_t].add(ys * slot_g[:, None].astype(ys.dtype))

def trunk_layer(x, mods, lp, s0_f, s0_b, ctx_k, ctx_v):
    sh1, sc1, g1, sh2, sc2, g2 = mods
    h = rmsnorm(x, lp["norm1"]) * (1.0 + sc1) + sh1
    mix, k_c, v_c, s_f, s_b = token_mixer(h, lp, s0_f, s0_b, ctx_k, ctx_v)
    x = x + g1 * mix
    h = rmsnorm(x, lp["norm2"]) * (1.0 + sc2) + sh2
    B, T, D = h.shape
    x = x + g2 * routed_ffn(h.reshape(B * T, D), lp).reshape(B, T, D)
    return x, k_c, v_c, s_f, s_b

def setup_inputs(seed: int = 0) -> dict:
    key = jax.random.key(seed)
    keys = list(jax.random.split(key, 40))

    def nrm(shape, scale):
        return scale * jax.random.normal(keys.pop(), shape, jnp.float32)

    def gain(shape):
        return 1.0 + nrm(shape, 0.05)

    L = DEPTH
    return {
        "x_prompt": nrm((BATCH, SEQ, D_MODEL), 1.0),
        "x_sample": nrm((DEC_BATCH, DEC_SEQ, D_MODEL), 1.0),
        "cache_k": nrm((DEC_BATCH, L, PAST_LEN, N_KV, HEAD_DIM), 1.0),
        "cache_v": nrm((DEC_BATCH, L, PAST_LEN, N_KV, HEAD_DIM), 1.0),
        "state_rwkv_fwd": nrm((DEC_BATCH, L, H_R, HEAD_R, HEAD_R), 0.5),
        "state_rwkv_bwd": nrm((DEC_BATCH, L, H_R, HEAD_R, HEAD_R), 0.5),
        "c": nrm((DEC_BATCH, D_MODEL), 1.0),
        "c_ctx": nrm((D_MODEL,), 1.0),
        "w_ada": nrm((L, D_MODEL, 6 * D_MODEL), 0.5 * D_MODEL ** -0.5),
        "b_ada": nrm((L, 6 * D_MODEL), 0.02),
        "norm1": gain((L, D_MODEL)),
        "norm2": gain((L, D_MODEL)),
        "w_in": nrm((L, D_MODEL, IN_COLS), D_MODEL ** -0.5),
        "rw_w0": jax.random.uniform(keys.pop(), (L, 2, D_R), jnp.float32, -6.0, 1.0),
        "rw_w2": nrm((L, 2, DECAY_RANK, D_R), 0.5 * DECAY_RANK ** -0.5),
        "rw_a0": nrm((L, 2, D_R), 0.5),
        "rw_a2": nrm((L, 2, AAA_RANK, D_R), 0.5 * AAA_RANK ** -0.5),
        "rw_g2": nrm((L, GATE_RANK, D_R), GATE_RANK ** -0.5),
        "rw_kk": 0.85 + nrm((L, D_R), 0.05),
        "rw_ka": gain((L, D_R)),
        "rw_rk": nrm((L, H_R, HEAD_R), 0.1),
        "rw_ln_w": gain((L, D_R)),
        "rw_ln_b": nrm((L, D_R), 0.02),
        "q_norm": gain((L, HEAD_DIM)),
        "k_norm": gain((L, HEAD_DIM)),
        "w_up_r": nrm((L, D_R, D_MODEL), D_R ** -0.5),
        "w_up_a": nrm((L, D_A, D_MODEL), D_A ** -0.5),
        "w_out": nrm((L, D_MODEL, D_MODEL), D_MODEL ** -0.5),
        "w_router": nrm((L, D_MODEL, N_EXPERTS), D_MODEL ** -0.5),
        "b_router": nrm((L, N_EXPERTS), 0.01),
        "w_moe_in": nrm((L, N_EXPERTS, D_MODEL, 2 * D_FF), D_MODEL ** -0.5),
        "b_moe_in": nrm((L, N_EXPERTS, 2 * D_FF), 0.02),
        "w_moe_out": nrm((L, N_EXPERTS, D_FF, D_MODEL), D_FF ** -0.5),
        "b_moe_out": nrm((L, N_EXPERTS, D_MODEL), 0.02),
        "norm_f": gain((D_MODEL,)),
    }

def reference(x_prompt, x_sample, cache_k, cache_v, state_rwkv_fwd, state_rwkv_bwd, c, c_ctx,
              w_ada, b_ada, norm1, norm2, w_in, rw_w0, rw_w2, rw_a0, rw_a2, rw_g2, rw_kk, rw_ka,
              rw_rk, rw_ln_w, rw_ln_b, q_norm, k_norm, w_up_r, w_up_a, w_out, w_router, b_router,
              w_moe_in, b_moe_in, w_moe_out, b_moe_out, norm_f):
    x_ctx, x_lat = x_prompt, x_sample
    new_k, new_v, new_sf, new_sb = [], [], [], []
    for l in range(DEPTH):
        lp = dict(norm1=norm1[l], norm2=norm2[l], w_in=w_in[l], rw_w0=rw_w0[l], rw_w2=rw_w2[l],
                  rw_a0=rw_a0[l], rw_a2=rw_a2[l], rw_g2=rw_g2[l], rw_kk=rw_kk[l], rw_ka=rw_ka[l],
                  rw_rk=rw_rk[l], rw_ln_w=rw_ln_w[l], rw_ln_b=rw_ln_b[l], q_norm=q_norm[l],
                  k_norm=k_norm[l], w_up_r=w_up_r[l], w_up_a=w_up_a[l], w_out=w_out[l],
                  w_router=w_router[l], b_router=b_router[l], w_moe_in=w_moe_in[l],
                  b_moe_in=b_moe_in[l], w_moe_out=w_moe_out[l], b_moe_out=b_moe_out[l])
        mods_ctx = adaln(c_ctx[None, :], w_ada[l], b_ada[l])
        mods_lat = adaln(c, w_ada[l], b_ada[l])
        zeros = jnp.zeros((x_ctx.shape[0], H_R, HEAD_R, HEAD_R), jnp.float32)
        x_ctx, k_l, v_l, sf_l, sb_l = trunk_layer(x_ctx, mods_ctx, lp, zeros, zeros, None, None)
        x_lat, _, _, _, _ = trunk_layer(x_lat, mods_lat, lp, state_rwkv_fwd[:, l], state_rwkv_bwd[:, l],
                                        cache_k[:, l], cache_v[:, l])
        new_k.append(k_l)
        new_v.append(v_l)
        new_sf.append(sf_l)
        new_sb.append(sb_l)
    y_prompt = rmsnorm(x_ctx, norm_f)
    y_sample = rmsnorm(x_lat, norm_f)
    new_cache_k = jnp.stack(new_k, axis=1)
    new_cache_v = jnp.stack(new_v, axis=1)
    new_state_fwd = jnp.stack(new_sf, axis=1)
    new_state_bwd = jnp.stack(new_sb, axis=1)
    return (y_prompt, y_sample, new_cache_k, new_cache_v, new_state_fwd, new_state_bwd)


_drawn_inputs = setup_inputs


def setup_inputs(seed=0):
    import zlib

    import numpy as np

    out = dict(_drawn_inputs(seed))
    spreads = {}
    factors = {'cache_k': 4.91,
     'cache_v': 4.908,
     'state_rwkv_fwd': 8.0,
     'state_rwkv_bwd': 7.99,
     'rw_ln_w': 7.944,
     'rw_ln_b': 35.625,
     'q_norm': 8.0,
     'b_router': 9.616,
     'b_moe_in': 8.0,
     'b_moe_out': 21.612}
    for name, (base, spread) in spreads.items():
        noise = np.random.default_rng([zlib.crc32(name.encode()), seed]).standard_normal(out[name].shape)
        drawn = base * np.exp(spread * noise) if base else spread * noise
        out[name] = __import__('jax').numpy.asarray(drawn.astype(out[name].dtype))
    for name, factor in factors.items():
        out[name] = (out[name] * factor).astype(out[name].dtype)
    return out
```

```python
from contextlib import ExitStack

import concourse.bass as bass
from concourse import mybir
import numpy as np

F32 = mybir.dt.float32
BF16 = mybir.dt.bfloat16
I32 = mybir.dt.int32
U32 = mybir.dt.uint32
U16 = mybir.dt.uint16
ALU = mybir.AluOpType
ACT = mybir.ActivationFunctionType
X = mybir.AxisListType.X

P = 128
D = 1024
KC = D // P
NT = 3
DR = 512
HR = 8
HD = 64
RANK = 64
NHQ = 8
NKV = 2
NE = 32
TOPK = 4
FF = 1024
PAST = 128
EPS = 1e-6
GN_EPS = 64e-5
KK_EPS = 1e-12
ALPHA = 1.702
LIMIT = 7.0
CDEC = float(np.exp(-0.5))
SCALE = HD ** -0.5

ZR, ZK, ZV, ZWD, ZAD, ZGD, ZQ = 0, 512, 1024, 1536, 1664, 1792, 1920
ZKA, ZVA, ZW = 2432, 2560, 2688
CH = 512
ZCHUNKS = [(c, min(CH, ZW - c)) for c in range(0, ZW, CH)]
GCHUNKS = [(ZW + c, CH) for c in range(0, 2 * D, CH)]
NZ = len(ZCHUNKS)
ADA = 6 * D // CH
ADA1 = 4
NQK = NHQ + NKV
LEVELS = 7
NB = 3
QMAX = NE * NB
NEXTRA = NT * P * TOPK // (P + 1)
NBMAX = NE + NEXTRA
SLOT = KC * CH


def constants():
    s = np.arange(P)[:, None]
    t = np.arange(P)[None, :]
    out = {}
    mid = P // 2 - 1
    inc_f = (s <= t).astype(np.float32) - (s <= mid)
    exc_f = (s < t).astype(np.float32) - (s <= mid)
    inc_b = (s >= t).astype(np.float32) - (s > mid)
    exc_b = (s > t).astype(np.float32) - (s > mid)
    out["c_ident"] = np.eye(P, dtype=np.float32)
    out["c_cum"] = np.stack([inc_f, exc_f, inc_b, exc_b], 1).reshape(P, 4 * P).astype(np.float32)
    first = np.arange(P) <= mid
    col = np.stack([first, ~first, ~first, first], 1).astype(np.float32)
    out["c_col"] = col
    gram = []
    for d in range(2):
        strict = (s < t) if d == 0 else (s > t)
        incl = (s <= t) if d == 0 else (s >= t)
        gram.append(np.concatenate([strict, incl, strict, incl], 1))
    out["c_gram"] = np.concatenate(gram, 1).astype(np.uint16) * np.uint16(0x3F80)
    lev = []
    for d in range(2):
        for l in range(LEVELS):
            same = (s >> (l + 1)) == (t >> (l + 1))
            sb, tb = (s >> l) & 1, (t >> l) & 1
            lev.append(same & ((sb == 0) & (tb == 1) if d == 0 else (sb == 1) & (tb == 0)))
    out["c_level"] = np.concatenate(lev, 1).astype(np.uint16) * np.uint16(0x3F80)
    inv = 10000.0 ** (-np.arange(0, HD // 2, 2, dtype=np.float32) / np.float32(HD // 2))
    pos = np.arange(2 * P)
    row, colp = (pos // 64).astype(np.float32), (pos % 64).astype(np.float32)
    ang = np.stack([row[:, None] * inv[None], colp[:, None] * inv[None]], 1).astype(np.float32)
    cs = np.stack([np.cos(ang), np.sin(ang)], 1).astype(np.float32)
    out["c_rope"] = cs.reshape(2, P, 64).transpose(1, 0, 2).reshape(P, 128).copy()
    out["c_rank"] = np.concatenate([(s < t), np.ones((P, P))], 1).astype(np.float32)
    out["c_tok"] = (np.arange(P)[:, None] + P * np.arange(NT)[None]).astype(np.float32)
    out["c_iota"] = np.broadcast_to(np.arange(P, dtype=np.float32), (P, P)).copy()
    q = np.arange(P)
    thr = np.where(q < NE, -1.0, np.where(q < 2 * NE, P, 2 * P)).astype(np.float32)
    out["c_q"] = np.stack([q, q % NE, thr, np.ones(P)], 1).astype(np.float32)
    sel = np.zeros((QMAX, NE, P), np.uint16)
    for e in range(NE):
        sel[e::NE, e, :] = 0x3F80
    out["c_sel"] = sel.reshape(QMAX, NE * P)
    return out


_CONST = constants()


def build(nc, a, o):
    ctx = ExitStack()
    with ctx:
        sb = lambda n, s, d=F32: ctx.enter_context(nc.sbuf_tensor(n, s, d))
        sem = lambda n: ctx.enter_context(nc.semaphore(n))
        dram = lambda n, s: nc.dram_tensor(n, s, F32, kind="Internal").ap()

        mods_d = dram("mods_d", (2, 6 * D))
        gates_d = dram("gates_d", (NT, P, 2 * D))
        h2_d = dram("h2_d", (NT * P, D))
        rows_d = dram("rows_d", (NBMAX * P, D))

        ring = sb("ring", [P, 3 * SLOT])
        zbuf = sb("zbuf", [P, NT, ZW])
        ky = sb("ky", [P, 2 * NT * DR])
        rowc = sb("rowc", [P, 7 * DR])
        work = sb("work", [P, 20480])
        smallw = sb("smallw", [P, 3 * DR + KC * NE])
        turned = sb("turned", [P, 3, NT * P])
        ident = sb("ident", [P, P])
        cum = sb("cum", [P, 4, P])
        colm = sb("colm", [P, 4])
        gram16 = sb("gram16", [P, 2 * 4 * P], U16)
        level16 = sb("level16", [P, 2 * LEVELS * P], U16)
        gramm = gram16[:, :].bitcast(BF16).rearrange("p (d n) -> p d n", d=2)
        levelm = level16[:, :].bitcast(BF16).rearrange("p (l n) -> p l n", n=P)
        rope = sb("rope", [P, 2, 2, 2, 16])
        condc = sb("condc", [16, P])
        condf = sb("condf", [P, 2, 16])
        condT = sb("condT", [P, KC, 2])
        stat = sb("stat", [P, 64])
        half = sb("half", [P, 16])
        bonus = sb("bonus", [P, NT, 2, HR])
        states = sb("states", [P, 2, 4, HD])
        sfin = sb("sfin", [P, 4, HD])
        stout = sb("stout", [HD, 4 * P])
        tab = sb("tab", [1, 2 * P + 1], I32)
        slots = sb("slots", [P, 1], U32)
        dest = sb("dest", [P, NT * TOPK], U32)
        gate = sb("gate", [P, NT, TOPK])

        def at(buf, start, *shape, rows=P):
            n = int(np.prod(shape))
            v = buf[0:rows, start:start + n]
            if len(shape) == 1:
                return v
            names = "abcd"[:len(shape)]
            return v.rearrange(f"p ({' '.join(names)}) -> p {' '.join(names)}",
                               **{names[i]: shape[i] for i in range(len(shape))})

        ring_slot = [at(ring, i * SLOT, KC, CH) for i in range(3)]
        kkn = at(ky, 0, NT, DR)
        yrw = at(ky, NT * DR, NT, DR)
        w0b, a0b = at(rowc, 0, 2, DR), at(rowc, 2 * DR, 2, DR)
        kkb, kab, rkb = (at(rowc, i * DR, DR) for i in (4, 5, 6))
        w2s, a2s, g2s = (at(smallw, i * DR, DR) for i in (0, 1, 2))
        wrout = at(smallw, 3 * DR, KC, NE)
        twT, adT, sgT = turned[:, 0, :], turned[:, 1, :], turned[:, 2, :]
        hT = at(work, 0, KC, NT * P)
        modrow = at(work, 3072, 6 * D, rows=2)
        nrm = at(work, 9216, D)
        scb, shb = at(work, 10240, 2, D), at(work, 12288, 2, D)
        xb = at(work, 14336, NT, D)
        junk = at(work, 17408, D)
        gst = at(work, 18432, 4, CH)
        QT, KT = at(work, 0, 4, NT * P), at(work, 1536, 2, 4 * P)
        qk = at(work, 9216, NT, NQK, HD)
        rt = at(work, 11136, 4, NQK * 32)
        gqk = at(work, 12416, 2, HD)
        kdup = at(work, 13056, 4, HD)
        ckv = at(work, 13312, 2, NKV * HD)
        prob = at(work, 13568, 2, 3 * P)
        probT = at(work, 14336, 2, 3 * P)
        sq = at(work, 15104, NQK * HD)
        LW, AA, T1, T2 = (at(work, i * DR, DR) for i in range(4))
        ER, EQ, EN = (at(work, 2048 + i * DR, DR) for i in range(3))
        RQ = at(work, 3584, 2, DR)
        BT_, KT_ = at(work, 4608, DR), at(work, 5120, DR)
        KD = at(work, 5632, DR)
        QRT = at(work, 6144, 4, 2, P)
        BTT, KTT = at(work, 7168, 4, P), at(work, 7680, 4, P)
        AM = at(work, 8192, HR, 4, P)
        ATL = [[at(work, 12288 + (2 * g + b) * DR, 4, P) for b in range(2)] for g in range(2)]
        XM = [at(work, 14336 + g * 3 * DR, 4, P) for g in range(2)]
        XT = [at(work, 14848 + g * 3 * DR, 4, P) for g in range(2)]
        PM = [at(work, 15360 + g * 3 * DR, 4, P) for g in range(2)]
        GM, U1, U2, UU = ([at(work, 17408 + g * 1024 + i * 256, 4, HD) for g in range(2)] for i in range(4))
        S0P = at(work, 19456, 4, 2, HD)
        stin = at(work, 19712, 4 * P, rows=HD)
        ecol = at(work, 20224, 4, 2)
        yrT, yaT = at(work, 0, 4, NT * P), at(work, 1536, 4, NT * P)
        gld = at(work, 3072, 2 * D)
        mg, mg2 = at(work, 5120, D), at(work, 6144, D)
        mT = at(work, 7168, KC, NT * P)
        lnw, lnb = at(work, 10240, DR), at(work, 10752, DR)
        yc, ysq = at(work, 11264, DR), at(work, 11776, DR)
        x1 = at(ky, 0, NT, D)
        xr2 = at(work, 12288, D)
        g1b = at(work, 13312, D)
        n2 = at(work, 14336, D)
        sc2 = at(work, 15360, D)
        sh2 = at(work, 16384, D)
        h2 = at(work, 17408, D)
        h2T = at(work, 18432, KC, P)
        wslot = ring_slot + [at(work, i * SLOT, KC, CH) for i in range(3)]
        w2slot = [at(work, (i + 1) * SLOT, 4, D) for i in range(2)]
        jk = zbuf[:, :, :].rearrange("p a b -> p (a b)")[:, 5120:6144]
        zf = zbuf[:, :, :].rearrange("p a b -> p (a b)")
        xg, act, ysb = zf[:, 0:1024], zf[:, 1024:2048], zf[:, 2048:3072]
        xT = zf[:, 3072:4096].rearrange("p (k t) -> p k t", k=KC)
        actT = zf[:, 4096:5120].rearrange("p (k t) -> p k t", k=KC)
        gl, th, uu = zf[:, 5120:5632], zf[:, 5632:6144], zf[:, 6144:6656]
        cmp = zf[:, 6656:7040].rearrange("p (j t) -> p j t", j=NT)
        rankm = zf[:, 7040:7328].rearrange("p (j q) -> p j q", j=NT)
        crank, iota = zf[:, 7328:7584], zf[:, 7584:7712]
        ctok, cq = zf[:, 7712:7715], zf[:, 7716:7720]
        brow = zf[:, 7720:7752]
        selm = zf[:, 7752:7848].rearrange("p (j e) -> p j e", j=NT)
        lgt = zf[:, 7848:7944].rearrange("p (j e) -> p j e", j=NT)
        mx8 = zf[:, 4096:4120].rearrange("p (j k) -> p j k", j=NT)
        ix8 = zf[:, 4120:4144].bitcast(U32).rearrange("p (j k) -> p j k", j=NT)
        ixf, rkf = zf[:, 4144:4156], zf[:, 4156:4168]
        pcol, acol, s12 = zf[0:QMAX, 4168:4169], zf[0:QMAX, 4169:4170], zf[:, 4170:4182]
        exd = zf[:, 4182:4194].rearrange("p (j k) -> p j k", j=NT)
        sum3 = zf[:, 4194:4197]
        rkm = zf[:, 4224:4320].rearrange("p (j e) -> p j e", j=NT)
        rsel = zf[:, 4320:4416].rearrange("p (j e) -> p j e", j=NT)
        aspread, posb = zf[0:QMAX, 5376:5504], zf[:, 5504:5600]
        pdif, d12 = zf[:, 5600:5664], [zf[:, 5664:5676], zf[:, 5676:5688]]
        lsto = zf[0:QMAX, 4416:4544]
        onehot = zf[:, 4608:4992].rearrange("p (k e) -> p k e", e=NE)
        ohr = zf[:, 4992:5376].rearrange("p (k e) -> p k e", e=NE)
        b3 = at(rowc, 0, 1536).bitcast(BF16)
        selc = at(rowc, 1536, 2048).bitcast(BF16).rearrange("p (e t) -> p e t", e=NE)
        bias32 = at(work, 12288, 3072)
        bt0, bt1 = at(work, 15360, CH), at(work, 15872, CH)
        btb = at(work, 16384, CH).bitcast(BF16)[:, 0:CH]
        ygat = [at(work, 12288 + i * D, D) for i in range(4)]
        facc, nfb = at(work, 16384, D), at(work, 18432, D)
        g2b = [at(work, 17408, D), at(work, 19456, D)]

        pb = [ctx.enter_context(nc.psum_tensor(f"bank{i}", [P, 512], F32)) for i in range(8)]
        B = [b[:, :] for b in pb]

        names = """ident cond bada n1 modd modb1 ssq rstd htok htr hTa hTv wdone zmm zA zV cons2 cons3
        cachekv nkv anorm arstd aqk kdupd qtr ktr qTa kTv smm nmax prob rinv ptr ptc pv ya tg sgd ttr tcA
        tcV kkss kkr kkd stld sttr stev lora lt1 ltanh lw lcum lexp rqd bkd ttr4 rqT bkT s0p gram am yout
        yrd twod st2 sftr sfcp sfout lnld gld gps yfin ytr yTc upm mrg mtr mTc wout xr g1l x1s n2l h2s
        h2out h2tr h2Tc lg cons4 exa exb b32 b3d selld cmpd idxm idxc xgd xtm xtc hmm gld2 thd actd atm atc
        w2m ymm yc yo ygc fin fout fld chain chain2 gpn zset zfill chain2v modrow condq routeq""".split()
        S = {n: sem("s_" + n) for n in names}
        s_wld = [sem(f"s_wld{i}") for i in range(3)]
        s_xl = [sem(f"s_xl{j}") for j in range(NT)]
        s_gst = [sem(f"s_gst{i}") for i in range(4)]
        s_at = [sem(f"s_at{g}") for g in range(2)]
        s_p = [sem(f"s_p{g}") for g in range(2)]
        s_pc = [sem(f"s_pc{g}") for g in range(2)]
        s_d = [sem(f"s_d{g}") for g in range(2)]
        s_x = [sem(f"s_x{g}") for g in range(2)]
        s_u = [sem(f"s_u{g}") for g in range(2)]
        s_uc = [sem(f"s_uc{g}") for g in range(2)]
        s_es = [sem(f"s_es{i}") for i in range(6)]
        s_yg = [sem(f"s_yg{i}") for i in range(4)]

        stream = [("ada", m) for m in range(ADA1)] + [("in", m) for m in range(NZ + 4)]
        stream += [("ada", m) for m in range(ADA1, ADA)] + [("upr", 0), ("upa", 0), ("out", 0), ("out", 1)]
        turn = {k: i for i, k in enumerate(stream)}

        def landed(eng, key):
            i = turn[key]
            eng.wait_ge(s_wld[i % 3], 16 * (i // 3 + 1))

        zunits = [(m, j) for m in range(NZ + 4) for j in range(NT)]

        def z_evacuated(eng, i):
            n = NZ * NT
            if i >= n:
                eng.wait_ge(S["zA"], n // 2 + i - n + 1)
            elif i % 2 == 0:
                eng.wait_ge(S["zA"], i // 2 + 1)
            else:
                eng.wait_ge(S["zV"], i // 2 + 1)

        aunits = [(j, h) for j in range(NT) for h in range(NHQ)]
        units = [(0, 0), (1, 2), (0, 1), (1, 1), (0, 2), (1, 0)]
        NU = len(units)
        CTX = [0, 5]
        LAT = [2, 1]

        LAST = [4, 3]
        lat_index = [sum(units[v][1] > 0 for v in range(u)) for u in range(NU)]
        st_index = [2 * sum(v not in LAST for v in range(u)) for u in range(NU)]
        gbank = [0, 1, 7, 2, 3, 4, 5, 6]

        def z_multiplied(eng, i):
            m, j = zunits[i]
            if j == NT - 1:
                eng.wait_ge(S["wdone"], turn["in", m] + 1)
            else:
                eng.wait_ge(S["zmm"], (NT - 1) * m + j + 1)

        flat = lambda name: a[name].rearrange("o d n -> o (d n)")
        cons2 = [
            (cum[:, :, :].rearrange("p a b -> p (a b)"), a["c_cum"]), (colm[:, :], a["c_col"]),
            (gram16[:, :], a["c_gram"]), (level16[:, :], a["c_level"]),
            (rope[:, :, :, :, :].rearrange("p a b c d -> p (a b c d)"), a["c_rope"]),
            (at(rowc, 0, 2 * DR), flat("rw_w0").broadcast_to([P, 2 * DR])),
            (at(rowc, 2 * DR, 2 * DR), flat("rw_a0").broadcast_to([P, 2 * DR])),
            (kkb, a["rw_kk"].broadcast_to([P, DR])), (kab, a["rw_ka"].broadcast_to([P, DR])),
            (rkb, flat("rw_rk").broadcast_to([P, DR])),
            (w2s, a["rw_w2"].rearrange("o d r n -> (o d r) n")),
            (a2s, a["rw_a2"].rearrange("o d r n -> (o d r) n")),
            (g2s, a["rw_g2"].rearrange("o r n -> (o r) n")),
            (wrout, a["w_router"].rearrange("o (k p) n -> p (o k) n", p=P)),
        ]
        NCONS2, NCONS3, NCONS4 = len(cons2), 2, 5

        block = ctx.enter_context(nc.Block())

        def link(eng, chain, ins, base=0):
            chain[0] += 1
            ins.then_inc(chain[1], 1)
            eng.wait_ge(chain[1], base + chain[0])

        @block.sync
        def _(sp):
            sp.dma_start(condc[0:8, :], a["c_ctx"].rearrange("(k p) -> k p", p=P)).then_inc(S["cond"], 16)
            sp.dma_start(condc[8:16, :], a["c"].rearrange("o (k p) -> (o k) p", p=P)).then_inc(S["cond"], 16)
            sp.dma_start(ident[:, :], a["c_ident"]).then_inc(S["ident"], 16)
            sp.dma_start(modrow, a["b_ada"].broadcast_to([2, 6 * D])).then_inc(S["bada"], 16)

            def weights(key):
                i = turn[key]
                kind, m = key
                if key == ("out", 1):
                    sp.wait_ge(S["upm"], NT)
                elif i >= 3:
                    sp.wait_ge(S["wdone"], i - 2)
                dst = ring_slot[i % 3]
                if kind == "ada":
                    src = a["w_ada"].rearrange("o (k p) n -> p (o k) n", p=P)[:, :, m * CH:(m + 1) * CH]
                elif kind == "in":
                    c, n = (ZCHUNKS + GCHUNKS)[m]
                    src = a["w_in"].rearrange("o (k p) n -> p (o k) n", p=P)[:, :, c:c + n]
                    dst = dst[:, :, 0:n]
                elif kind in ("upr", "upa"):
                    w = a["w_up_r" if kind == "upr" else "w_up_a"]
                    src = w.rearrange("o (k p) n -> p (o k) n", p=P)
                    dst = at(ring, (i % 3) * SLOT, 4, D)
                else:
                    src = a["w_out"].rearrange("o (k p) n -> p (o k) n", p=P)[:, :, m * CH:(m + 1) * CH]
                sp.dma_start(dst, src).then_inc(s_wld[i % 3], 16)

            weights(("ada", 0))
            weights(("ada", 1))
            weights(("ada", 2))
            for j in range(NT):
                src = a["x_prompt"][0] if j == 0 else a["x_sample"][0, (j - 1) * P:j * P, :]
                sp.dma_start(xb[:, j, :], src).then_inc(s_xl[j], 16)
            sp.dma_start(nrm, a["norm1"].broadcast_to([P, D])).then_inc(S["n1"], 16)
            weights(("ada", 3))
            weights(("in", 0))
            weights(("in", 1))
            sp.wait_ge(S["modrow"], ADA1)
            sp.dma_start(mods_d[:, 0:ADA1 * CH], modrow[:, 0:ADA1 * CH]).then_inc(S["modd"], 16)
            sp.wait_ge(S["modd"], 16)
            for i in range(2):
                sp.dma_start(shb[:, i, :], mods_d[i:i + 1, 0:D].broadcast_to([P, D])).then_inc(S["modb1"], 16)
                sp.dma_start(scb[:, i, :], mods_d[i:i + 1, D:2 * D].broadcast_to([P, D])).then_inc(S["modb1"], 16)
            for m in range(2, NZ + 4):
                weights(("in", m))
            for m in range(ADA1, ADA):
                weights(("ada", m))
            sp.wait_ge(S["modrow"], ADA)
            sp.dma_start(mods_d[:, ADA1 * CH:], modrow[:, ADA1 * CH:]).then_inc(S["modd"], 16)
            for key in (("upr", 0), ("upa", 0), ("out", 0), ("out", 1)):
                weights(key)

            w1d, w2d = a["w_moe_in"][0], a["w_moe_out"][0]
            w1cols = [0, FF, CH, FF + CH]

            def expert_chunk(e, c):
                if c < 4:
                    src = w1d[e].rearrange("o (k p) n -> p (o k) n", p=P)[:, :, w1cols[c]:w1cols[c] + CH]
                    return sp.dma_start(wslot[c], src)
                src = w2d[e].rearrange("o (k p) n -> p (o k) n", p=P)[:, 4 * (c - 4):4 * (c - 3), :]
                return sp.dma_start(w2slot[c - 4], src)

            sp.wait_ge(S["upm"], NT)
            sp.wait_ge(S["wout"], 2 * NT)
            for c in range(6):
                expert_chunk(slice(0, 1), c).then_inc(s_es[c], 16)
            sp.wait_ge(S["routeq"], 8)
            nblk = sp.value_load(tab[0:1, 2 * P:2 * P + 1], min_val=NE, max_val=NBMAX)
            with sp.Fori(1, nblk) as it:
                e = sp.value_load(tab[0:1, bass.ds(it + P, 1)], min_val=0, max_val=NE - 1)
                for c in range(4):
                    sp.wait_ge(S["hmm"], 4 * it + (c - 3))
                    expert_chunk(bass.ds(e, 1), c).then_inc(s_es[c], 16)
                for c in range(2):
                    sp.wait_ge(S["w2m"], 2 * it + (c - 1))
                    expert_chunk(bass.ds(e, 1), 4 + c).then_inc(s_es[4 + c], 16)

            for j in range(NT):
                sp.wait_ge(S["fin"], j + 1)
                dst = o["y_prompt"][0] if j == 0 else o["y_sample"][0, (j - 1) * P:j * P, :]
                sp.dma_start(dst, x1[:, j, :]).then_inc(S["fout"], 16)
            sp.wait_ge(S["fout"], 16 * NT)
            sp.wait_ge(S["nkv"], 32)
            sp.wait_ge(S["sfout"], 32)

        @block.gpsimd
        def _(gp):
            gp.memset(at(ky, 0, D), 0.0).then_inc(S["zset"], 1)
            gp.memset(half[:, :], -0.5).then_inc(S["chain2"], 1)
            gp.wait_ge(S["chain2"], 1)
            rs = ALU.pow
            for j in range(NT):
                gp.wait_ge(S["ssq"], j + 1)
                gp.tensor_tensor(stat[:, 8 + j:9 + j], stat[:, 4 + j:5 + j], half[:, 0:1], rs).then_inc(S["rstd"], 1)
            for j in range(NT):
                gp.wait_ge(S["anorm"], j + 1)
                gp.tensor_tensor(stat[:, 36:46], stat[:, 26:36], half[:, 0:10], rs).then_inc(S["arstd"], 1)
            for j in range(NT):
                gp.wait_ge(S["kkss"], j + 1)
                gp.tensor_tensor(stat[:, 16:24], stat[:, 8:16], half[:, 0:8], rs).then_inc(S["kkr"], 1)

            for u, (d, j) in enumerate(units):
                gp.wait_ge(S["kkd"], j + 1)
                gp.wait_ge(S["lexp"], 4 * u + 3)
                gp.tensor_tensor(RQ[:, 0, :], kkn[:, j, :], EQ, ALU.mult).then_inc(S["rqd"], 1)
                gp.tensor_tensor(RQ[:, 1, :], zbuf[:, j, ZR:ZR + DR], ER, ALU.mult).then_inc(S["rqd"], 1)

                def level(g, l):
                    if l == 0:
                        gp.wait_ge(S["am"], 8 * u + 4 * g + 4)
                    if l == 1 and u:
                        gp.wait_ge(s_p[g], 6 * u)
                    if l >= 2:
                        gp.wait_ge(s_p[g], 6 * u + l - 1)
                        gp.wait_ge(s_x[g], 6 * u + 1)
                    m = levelm[:, LEVELS * d + l:LEVELS * d + l + 1, :].broadcast_to([P, 4, P])
                    gp.tensor_tensor(ATL[g][l % 2], AM[:, 4 * g:4 * g + 4, 0, :], m, ALU.mult).then_inc(s_at[g], 1)

                for l in range(LEVELS):
                    for g in range(2):
                        level(g, l)
            for j in range(NT):
                gp.wait_ge(S["kkss"], NT + j + 1)
                gp.tensor_tensor(stat[:, 16:24], stat[:, 8:16], half[:, 0:8], rs).then_inc(S["kkr"], 1)
            for j in range(NT):
                gp.wait_ge(S["ssq"], NT + j + 1)
                gp.tensor_tensor(stat[:, 8 + j:9 + j], stat[:, 4 + j:5 + j], half[:, 0:1], rs).then_inc(S["rstd"], 1)

            def gather(count, prior):
                gp.wait_ge(S["idxc"], count)
                gp.wait_ge(S["h2out"], 16 * NT)
                if prior is not None:
                    gp.wait_ge(S["gpn"], prior)
                gp.tensor_tensor(half[:, 12:13], half[:, 13:14], half[:, 13:14], ALU.mult).then_inc(S["gpn"], 1)
                gp.indirect_dma_start(xg, None, h2_d, bass.IndirectOffsetOnAxis(ap=slots[:, 0:1], axis=0))\
                  .then_inc(S["xgd"], 16)

            gather(1, None)
            gp.wait_ge(S["routeq"], 8)
            nblk = gp.value_load(tab[0:1, 2 * P:2 * P + 1], min_val=NE, max_val=NBMAX)
            with gp.Fori(0, nblk) as it:
                gp.wait_ge(S["xtm"], 2 * it + 2)
                gather(it + 2, it + 1)
            gp.wait_ge(S["yo"], 16 * nblk + 16)
            gp.wait_ge(S["gpn"], nblk + 1)
            gp.tensor_tensor(half[:, 12:13], half[:, 13:14], half[:, 13:14], ALU.mult)
            for n in range(NT * TOPK):
                if n >= 4:
                    gp.wait_ge(S["ygc"], n - 3)
                else:
                    gp.wait_ge(S["b3d"], 1)
                gp.indirect_dma_start(ygat[n % 4], None, rows_d,
                                      bass.IndirectOffsetOnAxis(ap=dest[:, n:n + 1], axis=0))\
                  .then_inc(s_yg[n % 4], 16)
                if n % TOPK == TOPK - 1:
                    j = n // TOPK
                    gp.wait_ge(S["ssq"], 2 * NT + j + 1)
                    gp.tensor_tensor(stat[:, 8 + j:9 + j], stat[:, 4 + j:5 + j], half[:, 0:1], rs).then_inc(S["rstd"], 1)

        @block.tensor
        def _(pe):
            def mm(out, l, r, start=True, stop=True):
                return pe.matmul(out, l, r, start=start, stop=stop)

            def mm_part(out, l, r, start=True, stop=True):
                return pe.matmul(out, l, r, start=start, stop=stop, skip_group_check=True)

            def tr(out, src, n=P):
                return pe.transpose(out, src, ident[0:n, 0:n])

            pe.wait_ge(S["cond"], 32)
            pe.wait_ge(S["ident"], 16)
            tr(B[7][:, 0:16], condc[:, :], 16).then_inc(S["condq"], 1)
            pe.wait_ge(S["condq"], 4)

            def modulation(m):
                landed(pe, ("ada", m))
                if m >= 2:
                    pe.wait_ge(S["modrow"], m - 1)
                for k in range(KC):
                    last = mm(B[6 + m % 2][0:2, :], condT[:, k, :], ring_slot[turn["ada", m] % 3][:, k, :],
                              k == 0, k == KC - 1)
                last.then_inc(S["wdone"], 1)

            for m in range(ADA1):
                modulation(m)
            for j in range(NT):
                pe.wait_ge(S["htok"], j + 1)
                if j == 2:
                    pe.wait_ge(S["hTa"], 1)
                    pe.wait_ge(S["hTv"], 1)
                for k in range(KC):
                    bank = B[2 * (j % 2) + k // 4]
                    last = tr(bank[:, (k % 4) * P:(k % 4 + 1) * P], xb[:, j, k * P:(k + 1) * P])
                    if k % 4 == 3:
                        last.then_inc(S["htr"], 1)
            pe.wait_ge(S["hTa"], NT)
            pe.wait_ge(S["hTv"], NT)
            for i, (m, j) in enumerate(zunits):
                n = (ZCHUNKS + GCHUNKS)[m][1]
                w = ring_slot[turn["in", m] % 3]
                if j == 0:
                    landed(pe, ("in", m))
                if i >= 6:
                    z_evacuated(pe, i - 6)
                for k in range(KC):
                    last = mm(B[i % 6][:, 0:n], hT[:, k, j * P:(j + 1) * P], w[:, k, 0:n], k == 0, k == KC - 1)
                last.then_inc(S["wdone"] if j == NT - 1 else S["zmm"], 1)
            for m in range(ADA1, ADA):
                modulation(m)
            for i in range(len(zunits) - 6, len(zunits)):
                z_evacuated(pe, i)
            pe.wait_ge(S["modrow"], ADA)

            for j in range(NT + 1):
                if j < NT:
                    pe.wait_ge(S["aqk"], j + 1)
                    if j:
                        pe.wait_ge(S["qTa"], j)
                    for c in range(4):
                        last = tr(B[0][:, c * P:(c + 1) * P], qk[:, j, 2 * c:2 * c + 2, :])
                    last.then_inc(S["qtr"], 1)
                pe.wait_ge(S["kdupd"], j + 1)
                if j:
                    pe.wait_ge(S["kTv"], j)
                for g in range(NKV):
                    last = tr(B[1][:, g * P:(g + 1) * P], kdup[:, 2 * g:2 * g + 2, :])
                last.then_inc(S["ktr"], 1)
            pe.wait_ge(S["qTa"], NT)
            pe.wait_ge(S["kTv"], NT + 1)

            def scores(n):
                j, h = aunits[n]
                base, c, g = HD * (h % 2), h // 2, h // (NHQ // NKV)
                keys = KT[base:base + HD, g, 0:P] if j == 0 else KT[base:base + HD, g, P:4 * P]
                if n >= 2:
                    pe.wait_ge(S["prob"], n - 1)
                mm(B[2 + n % 2][:, 0:P if j == 0 else 3 * P], QT[base:base + HD, c, j * P:(j + 1) * P], keys)\
                    .then_inc(S["smm"], 1)

            def turn_probs(n):
                nb = 1 if aunits[n][0] == 0 else 3
                pe.wait_ge(S["prob"], n + 1)
                if n >= 2:
                    pe.wait_ge(S["ptc"], n - 1)
                for b in range(nb):
                    last = tr(B[4 + n % 2][:, b * P:(b + 1) * P], prob[:, n % 2, b * P:(b + 1) * P])
                last.then_inc(S["ptr"], 1)

            def values(n):
                j, h = aunits[n]
                g = h // (NHQ // NKV)
                pe.wait_ge(S["ptc"], n + 1)
                if n >= 2:
                    pe.wait_ge(S["ya"], n - 1)
                if n == 0:
                    pe.wait_ge(S["cachekv"], 32)
                tiles = [0] if j == 0 else [1, 2, None]
                for b, t in enumerate(tiles):
                    v = ckv[:, 1, g * HD:(g + 1) * HD] if t is None else zbuf[:, t, ZVA + g * HD:ZVA + (g + 1) * HD]
                    last = mm(B[6 + n % 2][:, 0:HD], probT[:, n % 2, b * P:(b + 1) * P], v, b == 0, b == len(tiles) - 1)
                last.then_inc(S["pv"], 1)

            for n in range(len(aunits) + 2):
                if n < len(aunits):
                    scores(n)
                if 1 <= n <= len(aunits):
                    turn_probs(n - 1)
                if n >= 2:
                    values(n - 2)
            pe.wait_ge(S["ya"], len(aunits))

            pe.wait_ge(S["tg"], 2)
            pe.wait_ge(S["sgd"], 1)
            for i, c in enumerate((ZWD, ZAD, ZGD)):
                for j in range(NT):
                    last = tr(B[i][:, j * P:(j + 1) * P], zbuf[:, j, c:c + P])
                last.then_inc(S["ttr"], 1)
            for d in range(2):
                pe.wait_ge(S["stld"], 16 * (d + 1))
                if d:
                    pe.wait_ge(S["stev"], 1)
                for c in range(4):
                    last = tr(B[3][:, c * HD:(c + 1) * HD], stin[:, c * P:(c + 1) * P], HD)
                last.then_inc(S["sttr"], 1)
            pe.wait_ge(S["tcA"], 2)
            pe.wait_ge(S["tcV"], 1)
            pe.wait_ge(S["stev"], 2)
            pe.wait_ge(S["cons2"], 16 * NCONS2)

            for u, (d, j) in enumerate(units):
                lat = j > 0
                lo = 64 * d
                for i, (src, w) in enumerate(((twT, w2s), (adT, a2s))):
                    mm(B[i], src[lo:lo + 64, j * P:(j + 1) * P], w[lo:lo + 64, :]).then_inc(S["lora"], 1)
                pe.wait_ge(S["lw"], u + 1)
                pe.wait_ge(S["lt1"], 2 * u + 2)
                mm(B[0], cum[:, 2 * d, :], LW).then_inc(S["lcum"], 1)
                mm(B[1], cum[:, 2 * d + 1, :], LW).then_inc(S["lcum"], 1)
                for c in range(4):
                    last = mm(B[2][:, 2 * c:2 * c + 2], LW[:, c * P:(c + 1) * P], colm[:, 2 * d:2 * d + 2])
                last.then_inc(S["lcum"], 1)
                if u:
                    pe.wait_ge(S["yrd"], 2 * u)
                    pe.wait_ge(S["st2"], st_index[u])
                for i in range(4):
                    if i < 2:
                        pe.wait_ge(S["rqd"], 2 * u + i + 1)
                        src = RQ[:, i, :]
                    else:
                        pe.wait_ge(S["bkd"], 2 * u + i - 1)
                        src = (BT_, KT_)[i - 2]
                    for c in range(4):
                        last = tr(B[3 + i][:, c * P:(c + 1) * P], src[:, c * P:(c + 1) * P])
                    last.then_inc(S["ttr4"], 1)
                pe.wait_ge(S["rqT"], 2 * u + 2)
                pe.wait_ge(S["bkT"], 2 * u + 2)
                pe.wait_ge(S["lexp"], 4 * u + 4)
                for h in range(HR):
                    base, c = HD * (h % 2), h // 2
                    qr = QRT[base:base + HD, c, :, :]
                    mm(B[gbank[h]][:, 0:2 * P], BTT[base:base + HD, c, :], qr)
                    mm(B[gbank[h]][:, 2 * P:4 * P], KTT[base:base + HD, c, :], qr).then_inc(S["gram"], 1)
                pe.wait_ge(S["am"], 8 * u + 8)

                def heads(g):
                    return [(x, 4 * g + x) for x in range(4)]

                for l in range(LEVELS - 1):
                    for g in range(2):
                        bp = B[2 + 3 * g]
                        pe.wait_ge(s_at[g], 7 * u + l + 1)
                        if l:
                            pe.wait_ge(s_x[g], 6 * u + l)
                        for x, _ in heads(g):
                            last = mm(bp[:, x * P:(x + 1) * P], ATL[g][l % 2][:, x, :],
                                      XM[g][:, x, :] if l else ident[:, :])
                        last.then_inc(s_p[g], 1)
                    if l == 0:
                        continue
                    for g in range(2):
                        bd, bdt = B[3 + 3 * g], B[4 + 3 * g]
                        pe.wait_ge(s_pc[g], 5 * u + l)
                        for x, _ in heads(g):
                            if l < LEVELS - 2:
                                mm(bd[:, x * P:(x + 1) * P], XT[g][:, x, :], PM[g][:, x, :])
                            last = mm(bdt[:, x * P:(x + 1) * P], PM[g][:, x, :], XT[g][:, x, :])
                        last.then_inc(s_d[g], 1)
                vh = lambda h: zbuf[:, j, ZV + h * HD:ZV + (h + 1) * HD]
                if lat:
                    pe.wait_ge(S["s0p"], lat_index[u] + 1)
                for g in range(2):
                    for x, h in heads(g):
                        if lat and x % 2 == 0:
                            mm_part(B[2 + 3 * g][:, x * HD:(x + 2) * HD], QRT[:, h // 2, 0, :], S0P[:, h // 2, :, :],
                                    True, False)
                        last = mm_part(B[2 + 3 * g][:, x * HD:(x + 1) * HD], AM[:, h, 2, :], vh(h), not lat, True)
                    last.then_inc(s_u[g], 1)
                for g in range(2):
                    pe.wait_ge(s_uc[g], 4 * u + 1)
                    pe.wait_ge(s_x[g], 6 * u + 6)
                    for x, h in heads(g):
                        last = mm(B[3 + 3 * g][:, x * HD:(x + 1) * HD], XT[g][:, x, :], GM[g][:, x, :])
                    last.then_inc(s_u[g], 1)
                for g in range(2):
                    pe.wait_ge(s_uc[g], 4 * u + 2)
                    pe.wait_ge(s_at[g], 7 * u + 7)
                    for x, h in heads(g):
                        last = mm(B[4 + 3 * g][:, x * HD:(x + 1) * HD], ATL[g][0][:, x, :], U1[g][:, x, :])
                    last.then_inc(s_u[g], 1)
                for g in range(2):
                    pe.wait_ge(s_uc[g], 4 * u + 3)
                    for x, h in heads(g):
                        last = mm(B[2 + 3 * g][:, x * HD:(x + 1) * HD], XT[g][:, x, :], U2[g][:, x, :])
                    last.then_inc(s_u[g], 1)
                for g in range(2):
                    pe.wait_ge(s_uc[g], 4 * u + 4)
                    for x, h in heads(g):
                        out = B[3 + 3 * g][:, x * HD:(x + 1) * HD]
                        if lat and x % 2 == 0:
                            mm_part(B[3 + 3 * g][:, x * HD:(x + 2) * HD], QRT[:, h // 2, 1, :], S0P[:, h // 2, :, :],
                                    True, False)
                        mm_part(out, AM[:, h, 1, :], UU[g][:, x, :], not lat, False)
                        last = mm_part(out, AM[:, h, 3, :], vh(h), False, True)
                    last.then_inc(S["yout"], 1)
                    if u not in LAST:
                        for x, h in heads(g):
                            base = HD * (h % 2)
                            out = B[4 + 3 * g][base:base + HD, (x // 2) * HD:(x // 2 + 1) * HD]
                            mm(out, BT_[:, h * HD:(h + 1) * HD], UU[g][:, x, :], True, False)
                            last = mm(out, KT_[:, h * HD:(h + 1) * HD], vh(h), False, True)
                        last.then_inc(S["twod"], 1)
                if not lat:
                    pe.wait_ge(S["st2"], st_index[u] + 2)
                    for c in range(4):
                        last = tr(B[0][0:HD, c * P:(c + 1) * P], sfin[:, c, :])
                    last.then_inc(S["sftr"], 1)
                    pe.wait_ge(S["sfcp"], CTX.index(u) + 1)
            pe.wait_ge(S["yrd"], 2 * NU)

            for j in range(NT):
                if j:
                    pe.wait_ge(S["yfin"], j)
                mm(B[6], sgT[:, j * P:(j + 1) * P], g2s).then_inc(S["gps"], 1)
                pe.wait_ge(S["yfin"], j + 1)
                if j:
                    pe.wait_ge(S["yTc"], 2 * j)
                    pe.wait_ge(S["mTc"], 2 * j)
                for c in range(4):
                    last = tr(B[7][:, c * P:(c + 1) * P], yc[:, c * P:(c + 1) * P])
                last.then_inc(S["ytr"], 1)
                for c in range(4):
                    last = tr(B[5][:, c * P:(c + 1) * P], zbuf[:, j, ZQ + c * P:ZQ + (c + 1) * P])
                last.then_inc(S["ytr"], 1)
                pe.wait_ge(S["yTc"], 2 * j + 2)
                if j:
                    pe.wait_ge(S["mrg"], j)
                for i, (key, src) in enumerate((("upr", yrT), ("upa", yaT))):
                    if j == 0:
                        landed(pe, (key, 0))
                    w = at(ring, (turn[key, 0] % 3) * SLOT, 4, D)
                    for n in range(2):
                        for k in range(4):
                            last = mm(B[2 * i + n], src[:, k, j * P:(j + 1) * P], w[:, k, n * CH:(n + 1) * CH],
                                      k == 0, k == 3)
                last.then_inc(S["upm"], 1)
                pe.wait_ge(S["mrg"], j + 1)
                for k in range(KC):
                    last = tr(B[4 + k // 4][:, (k % 4) * P:(k % 4 + 1) * P], mg[:, k * P:(k + 1) * P])
                    if k % 4 == 3:
                        last.then_inc(S["mtr"], 1)
            pe.wait_ge(S["mTc"], 2 * NT)
            for j in range(NT):
                if j == 2:
                    pe.wait_ge(S["x1s"], 1)
                for n in range(2):
                    if j == 0:
                        landed(pe, ("out", n))
                    w = ring_slot[turn["out", n] % 3]
                    for k in range(KC):
                        last = mm(B[2 * (j % 2) + n], mT[:, k, j * P:(j + 1) * P], w[:, k, :], k == 0, k == KC - 1)
                    last.then_inc(S["wout"], 1)
            for j in range(NT):
                pe.wait_ge(S["h2s"], j + 1)
                if j:
                    pe.wait_ge(S["h2Tc"], 2 * j)
                for k in range(KC):
                    last = tr(B[4 + k // 4][:, (k % 4) * P:(k % 4 + 1) * P], h2[:, k * P:(k + 1) * P])
                    if k % 4 == 3:
                        last.then_inc(S["h2tr"], 1)
                pe.wait_ge(S["h2Tc"], 2 * j + 2)
                for k in range(KC):
                    last = mm(B[6][:, j * NE:(j + 1) * NE], h2T[:, k, :], wrout[:, k, :], k == 0, k == KC - 1)
                last.then_inc(S["lg"], 1)

            pe.wait_ge(S["routeq"], 1)
            pe.wait_ge(S["cons4"], 16 * NCONS4)
            for j in range(NT):
                for i in range(j + 1):
                    last = mm(B[7][:, j * NE:(j + 1) * NE], crank[:, 0:P] if i == j else crank[:, P:2 * P],
                              selm[:, i, :], i == 0, i == j)
            last.then_inc(S["routeq"], 1)
            for q in range(NB):
                for j in range(NT):
                    last = mm(B[5][q * NE:(q + 1) * NE, 0:1], selm[:, j, :], crank[:, P:P + 1], j == 0, j == NT - 1)
            last.then_inc(S["routeq"], 1)
            pe.wait_ge(S["routeq"], 4)
            mm(B[4][0:QMAX, 0:1], crank[0:QMAX, 0:QMAX], acol)
            mm(B[4][:, P:P + QMAX], aspread, crank[0:QMAX, 0:QMAX]).then_inc(S["routeq"], 1)
            pe.wait_ge(S["routeq"], 6)
            mm(B[3][0:1, 0:P], cq[0:QMAX, 0:1], lsto)
            mm(B[3][0:1, P:2 * P], cq[0:QMAX, 1:2], lsto)
            mm(B[3][0:1, 2 * P:2 * P + 1], acol, cq[0:QMAX, 3:4]).then_inc(S["routeq"], 1)

            hb, yb, t0, t1 = B[0:4], B[4:6], B[6], B[7]

            def list_tokens(count):
                pe.wait_ge(S["cmpd"], count)
                for j in range(NT):
                    last = mm(t1[:, 0:1], cmp[:, j, :], ctok[:, j:j + 1], j == 0, j == NT - 1)
                last.then_inc(S["idxm"], 1)

            def turn_rows(half_):
                for k in range(4 * half_, 4 * half_ + 4):
                    last = tr(t1[:, (k % 4) * P:(k % 4 + 1) * P], xg[:, k * P:(k + 1) * P])
                last.then_inc(S["xtm"], 1)

            list_tokens(1)
            pe.wait_ge(S["xgd"], 16)
            turn_rows(0)
            pe.wait_ge(S["xtc"], 1)
            turn_rows(1)
            pe.wait_ge(S["b3d"], 1)
            pe.wait_ge(S["selld"], 16)
            nblk = pe.value_load(tab[0:1, 2 * P:2 * P + 1], min_val=NE, max_val=NBMAX)
            with pe.Fori(0, nblk) as it:
                e = pe.value_load(tab[0:1, bass.ds(it + P, 1)], min_val=0, max_val=NE - 1)
                pe.wait_ge(S["xtc"], 2 * it + 2)
                for c in range(4):
                    if c % 2 == 0:
                        pe.wait_ge(S["actd"], 2 * it + (c // 2 + 1))
                    pe.wait_ge(s_es[c], 16 * it + 16)
                    mm(hb[c], selc[0:QMAX, bass.ds(e, 1), :].rearrange("p a t -> p (a t)"),
                       b3[0:QMAX, (c // 2) * CH + (c % 2) * FF:(c // 2) * CH + (c % 2) * FF + CH], True, False)
                    for k in range(KC):
                        last = mm(hb[c], xT[:, k, :], wslot[c][:, k, :], False, k == KC - 1)
                    last.then_inc(S["hmm"], 1)
                    if c == 0:
                        list_tokens(it + 2)
                pe.wait_ge(S["xgd"], 16 * it + 32)
                turn_rows(0)
                pe.wait_ge(S["actd"], 2 * it + 3)
                for k in range(4):
                    last = tr(t0[:, k * P:(k + 1) * P], act[:, k * P:(k + 1) * P])
                last.then_inc(S["atm"], 1)
                pe.wait_ge(S["xtc"], 2 * it + 3)
                turn_rows(1)
                pe.wait_ge(S["atc"], 2 * it + 1)
                pe.wait_ge(s_es[4], 16 * it + 16)
                pe.wait_ge(S["yc"], 2 * it + 2)
                for n in range(2):
                    mm(yb[n], selc[0:QMAX, bass.ds(e, 1), :].rearrange("p a t -> p (a t)"),
                       b3[0:QMAX, 2 * FF + n * CH:2 * FF + (n + 1) * CH], True, False)
                    for k in range(4):
                        last = mm(yb[n], actT[:, k, :], w2slot[0][:, k, n * CH:(n + 1) * CH], False, False)
                last.then_inc(S["w2m"], 1)
                pe.wait_ge(S["actd"], 2 * it + 4)
                for k in range(4):
                    last = tr(t0[:, k * P:(k + 1) * P], act[:, (4 + k) * P:(5 + k) * P])
                last.then_inc(S["atm"], 1)
                pe.wait_ge(S["atc"], 2 * it + 2)
                pe.wait_ge(s_es[5], 16 * it + 16)
                for n in range(2):
                    for k in range(4):
                        last = mm(yb[n], actT[:, 4 + k, :], w2slot[1][:, k, n * CH:(n + 1) * CH], False, k == 3)
                    last.then_inc(S["ymm"] if n == 0 else S["w2m"], 1)

        @block.scalar
        def _(sc):
            cp = lambda out, src, scale=1.0: sc.activation(out, src, ACT.Copy, scale=scale)
            sc.sem_inc(S["yc"], 2)
            sc.sem_inc(S["yo"], 16)
            sc.wait_ge(S["zset"], 1)
            for i in range(NEXTRA):
                sc.dma_start(rows_d[(NE + i) * P:(NE + i + 1) * P, :], at(ky, 0, D)).then_inc(S["zfill"], 16)
            for dst, src in cons2:
                sc.dma_start(dst, src).then_inc(S["cons2"], 16)
            sc.wait_ge(S["condq"], 2)
            sc.activation(condf[:, 1, :], condf[:, 0, :], ACT.Tanh, scale=0.5).then_inc(S["condq"], 1)
            for j in range(NT):
                sc.wait_ge(S["htr"], 2 * j + 1)
                cp(hT[:, 0:4, j * P:(j + 1) * P], B[2 * (j % 2)].rearrange("p (k t) -> p k t", k=4))\
                    .then_inc(S["hTa"], 1)
            sc.wait_ge(S["htok"], NT)
            for i, name in enumerate(("q_norm", "k_norm")):
                sc.dma_start(gqk[:, i, :], a[name].broadcast_to([P, HD])).then_inc(S["cons3"], 16)
            for i, name in enumerate(("cache_k", "cache_v")):
                sc.dma_start(ckv[:, i, :], a[name][0, 0].rearrange("t g d -> t (g d)")).then_inc(S["cachekv"], 16)
            for i, (m, j) in enumerate(zunits):
                if m < NZ and i % 2:
                    continue
                c, n = (ZCHUNKS + GCHUNKS)[m]
                z_multiplied(sc, i)
                if m < NZ:
                    cp(zbuf[:, j, c:c + n], B[i % 6][:, 0:n]).then_inc(S["zA"], 1)
                    continue
                r = i - NZ * NT
                if r >= 4:
                    sc.wait_ge(s_gst[r % 4], 16 * (r // 4))
                sc.activation(gst[:, r % 4, :], B[i % 6], ACT.Tanh, scale=0.5).then_inc(S["zA"], 1)
                z_evacuated(sc, i)
                sc.dma_start(gates_d[j, :, (m - NZ) * CH:(m - NZ + 1) * CH], gst[:, r % 4, :]).then_inc(s_gst[r % 4], 16)
            z_evacuated(sc, NZ * NT - 1)
            sc.activation(zbuf[:, :, ZWD:ZWD + P], zbuf[:, :, ZWD:ZWD + P], ACT.Tanh).then_inc(S["tg"], 1)
            sc.activation(zbuf[:, :, ZGD:ZGD + P], zbuf[:, :, ZGD:ZGD + P], ACT.Tanh, scale=0.5).then_inc(S["tg"], 1)
            for g in range(4):
                sc.wait_ge(s_gst[g], 48)
            for j in range(NT):
                sc.wait_ge(S["qtr"], j + 1)
                cp(QT[:, :, j * P:(j + 1) * P], B[0].rearrange("p (k t) -> p k t", k=4)).then_inc(S["qTa"], 1)
            sc.dma_start(o["new_cache_k"][0, 0].rearrange("t g d -> t (g d)"),
                         qk[:, 0, NHQ:NQK, :].rearrange("p g d -> p (g d)")).then_inc(S["nkv"], 16)
            sc.dma_start(o["new_cache_v"][0, 0].rearrange("t g d -> t (g d)"),
                         zbuf[:, 0, ZVA:ZVA + P]).then_inc(S["nkv"], 16)
            sc.dma_start(stin.rearrange("v (h k) -> v h k", h=HR),
                         a["state_rwkv_fwd"][0, 0].rearrange("h v k -> v h k")).then_inc(S["stld"], 16)

            def softmax(n):
                nk = P if aunits[n][0] == 0 else 3 * P
                sc.wait_ge(S["nmax"], n + 1)
                if n >= 2:
                    sc.wait_ge(S["ptr"], n - 1)
                    sc.wait_ge(S["rinv"], n - 1)
                sc.activation(prob[:, n % 2, 0:nk], B[2 + n % 2][:, 0:nk], ACT.Exp, scale=SCALE,
                              bias=stat[:, 50 + n % 2:51 + n % 2],
                              accum_out=stat[:, 52 + n % 2:53 + n % 2]).then_inc(S["prob"], 1)

            def weigh(n):
                j, h = aunits[n]
                sc.wait_ge(S["pv"], n + 1)
                sc.wait_ge(S["rinv"], n + 1)
                cp(zbuf[:, j, ZQ + h * HD:ZQ + (h + 1) * HD], B[6 + n % 2][:, 0:HD],
                   stat[:, 54 + n % 2:55 + n % 2]).then_inc(S["ya"], 1)

            for n in range(len(aunits) + 2):
                if n < len(aunits):
                    softmax(n)
                if n >= 2:
                    weigh(n - 2)

            for i, dst in ((0, twT), (2, sgT)):
                sc.wait_ge(S["ttr"], i + 1)
                cp(dst, B[i][:, 0:NT * P]).then_inc(S["tcA"], 1)
            sc.wait_ge(S["sttr"], 1)
            sc.dma_start(stin.rearrange("v (h k) -> v h k", h=HR),
                         a["state_rwkv_bwd"][0, 0].rearrange("h v k -> v h k")).then_inc(S["stld"], 16)
            for u, (d, j) in enumerate(units):
                for i, t in enumerate((T1, T2)):
                    sc.wait_ge(S["lt1"], 2 * u + i + 1)
                    sc.activation(t, t, ACT.Tanh, scale=0.5).then_inc(S["ltanh"], 1)
                sc.wait_ge(S["lcum"], 3 * u + 1)
                sc.activation(ER, B[0], ACT.Exp).then_inc(S["lexp"], 1)
                sc.activation(EN, B[0], ACT.Exp, scale=-1.0).then_inc(S["lexp"], 1)
                sc.wait_ge(S["lcum"], 3 * u + 2)
                sc.activation(EQ, B[1], ACT.Exp).then_inc(S["lexp"], 1)
                sc.wait_ge(S["lcum"], 3 * u + 3)
                sc.activation(ecol.rearrange("p a b -> p (a b)"), B[2][:, 0:8], ACT.Exp).then_inc(S["lexp"], 1)
                for i in range(2):
                    sc.wait_ge(S["ttr4"], 4 * u + i + 1)
                    cp(QRT[:, :, i, :], B[3 + i].rearrange("p (k t) -> p k t", k=4)).then_inc(S["rqT"], 1)
                for l in range(1, LEVELS - 1):
                    for g in range(2):
                        sc.wait_ge(s_p[g], 6 * u + l + 1)
                        cp(PM[g].rearrange("p a b -> p (a b)"), B[2 + 3 * g]).then_inc(s_pc[g], 1)
                for i, (dst, b) in enumerate(((GM, 2), (U1, 3), (U2, 4))):
                    for g in range(2):
                        sc.wait_ge(s_u[g], 4 * u + i + 1)
                        cp(dst[g].rearrange("p a b -> p (a b)"), B[b + 3 * g][:, 0:4 * HD]).then_inc(s_uc[g], 1)
                if u in CTX:
                    i = CTX.index(u)
                    sc.wait_ge(S["sftr"], i + 1)
                    if i:
                        sc.wait_ge(S["sfout"], 16)
                    cp(stout[:, :], B[0][0:HD, :]).then_inc(S["sfcp"], 1)
                    sc.wait_ge(S["sfcp"], i + 1)
                    dst = o["new_state_fwd" if d == 0 else "new_state_bwd"]
                    sc.dma_start(dst[0, 0].rearrange("h v k -> v h k"),
                                 stout[:, :].rearrange("v (h k) -> v h k", h=HR)).then_inc(S["sfout"], 16)
            sc.wait_ge(S["yrd"], 2 * NU)
            for dst, src in ((lnw, "rw_ln_w"), (lnb, "rw_ln_b")):
                sc.dma_start(dst, a[src].broadcast_to([P, DR])).then_inc(S["lnld"], 16)
            sc.dma_start(selc[0:QMAX, :, :].rearrange("p e t -> p (e t)").bitcast(U16), a["c_sel"]).then_inc(S["selld"], 16)
            sc.dma_start(gld, gates_d[0]).then_inc(S["gld"], 16)
            sc.dma_start(n2, a["norm2"].broadcast_to([P, D])).then_inc(S["n1"], 16)

            def cond_rows(i):
                sc.dma_start(g1b, mods_d[i:i + 1, 2 * D:3 * D].broadcast_to([P, D])).then_inc(S["g1l"], 16)

            def x_rows(j):
                src = a["x_prompt"][0] if j == 0 else a["x_sample"][0, (j - 1) * P:j * P, :]
                sc.dma_start(xr2, src).then_inc(S["xr"], 16)

            def norm2_rows(i):
                sc.dma_start(sh2, mods_d[i:i + 1, 3 * D:4 * D].broadcast_to([P, D])).then_inc(S["n2l"], 16)
                sc.dma_start(sc2, mods_d[i:i + 1, 4 * D:5 * D].broadcast_to([P, D])).then_inc(S["n2l"], 16)

            sc.wait_ge(S["modd"], 32)
            cond_rows(0)
            x_rows(0)
            norm2_rows(0)
            for j in range(NT):
                for i, dst in enumerate((yrT, yaT)):
                    sc.wait_ge(S["ytr"], 2 * j + i + 1)
                    cp(dst[:, :, j * P:(j + 1) * P], B[(7, 5)[i]].rearrange("p (k t) -> p k t", k=4)).then_inc(S["yTc"], 1)
                for i in range(2):
                    sc.wait_ge(S["mtr"], 2 * j + i + 1)
                    cp(mT[:, 4 * i:4 * i + 4, j * P:(j + 1) * P], B[4 + i].rearrange("p (k t) -> p k t", k=4), 0.5)\
                        .then_inc(S["mTc"], 1)
                if j + 1 < NT:
                    sc.wait_ge(S["mrg"], j + 1)
                    sc.dma_start(gld, gates_d[j + 1]).then_inc(S["gld"], 16)
            sc.wait_ge(S["yfin"], NT)
            for dst, src in ((crank, a["c_rank"]), (iota, a["c_iota"]), (ctok, a["c_tok"]), (cq, a["c_q"]),
                             (brow, a["b_router"].broadcast_to([P, NE]))):
                sc.dma_start(dst, src).then_inc(S["cons4"], 16)
            for j in range(1, NT):
                sc.wait_ge(S["x1s"], j)
                x_rows(j)
                if j == 1:
                    cond_rows(1)
            for j in range(NT):
                sc.wait_ge(S["h2s"], j + 1)
                sc.dma_start(h2_d[j * P:(j + 1) * P, :], h2).then_inc(S["h2out"], 16)
                if j == 0:
                    norm2_rows(1)
                for i in range(2):
                    sc.wait_ge(S["h2tr"], 2 * j + i + 1)
                    if j:
                        sc.wait_ge(S["lg"], j)
                    cp(h2T[:, 4 * i:4 * i + 4, :], B[4 + i].rearrange("p (k t) -> p k t", k=4)).then_inc(S["h2Tc"], 1)
            sc.wait_ge(S["exa"], 1)
            sc.activation(exd, exd, ACT.Exp).then_inc(S["exb"], 1)
            sc.wait_ge(S["lg"], NT)
            for q in range(NB):
                sc.dma_start(bias32[q * NE:(q + 1) * NE, 0:2 * FF], a["b_moe_in"][0]).then_inc(S["b32"], 16)
                sc.dma_start(bias32[q * NE:(q + 1) * NE, 2 * FF:3 * FF], a["b_moe_out"][0]).then_inc(S["b32"], 16)

            def listed(count):
                sc.wait_ge(S["idxm"], count)
                cp(slots[:, :], B[7][:, 0:1]).then_inc(S["idxc"], 1)

            def rows_turned(half_, count):
                sc.wait_ge(S["xtm"], count)
                cp(xT[:, 4 * half_:4 * half_ + 4, :], B[7].rearrange("p (k t) -> p k t", k=4)).then_inc(S["xtc"], 1)

            listed(1)
            rows_turned(0, 1)
            rows_turned(1, 2)
            sc.wait_ge(S["h2out"], 16 * NT)
            for dst, src in ((nfb, a["norm_f"].rearrange("(o n) -> o n", o=1)), (g2b[0], mods_d[0:1, 5 * D:6 * D]),
                             (g2b[1], mods_d[1:2, 5 * D:6 * D])):
                sc.dma_start(dst, src.broadcast_to([P, D])).then_inc(S["fld"], 16)
            sc.wait_ge(S["routeq"], 8)
            nblk = sc.value_load(tab[0:1, 2 * P:2 * P + 1], min_val=NE, max_val=NBMAX)
            rows_q = rows_d.rearrange("(q t) n -> q t n", t=P)
            with sc.Fori(0, nblk) as it:

                def sigmoid(h):
                    sc.wait_ge(S["gld2"], 2 * it + (h + 1))
                    sc.activation(th, gl, ACT.Tanh, scale=ALPHA / 2).then_inc(S["thd"], 1)

                def act_turned(h):
                    sc.wait_ge(S["atm"], 2 * it + (h + 1))
                    cp(actT[:, 4 * h:4 * h + 4, :], B[6].rearrange("p (k t) -> p k t", k=4), 0.5).then_inc(S["atc"], 1)

                sigmoid(0)
                sc.wait_ge(S["xgd"], 16 * it + 16)
                listed(it + 2)
                sigmoid(1)
                rows_turned(0, 2 * it + 3)
                act_turned(0)
                rows_turned(1, 2 * it + 4)
                act_turned(1)
                sc.wait_ge(S["w2m"], 2 * it + 2)
                sc.wait_ge(S["yo"], 16 * it + 16)
                cp(ysb[:, CH:D], B[5]).then_inc(S["yc"], 1)
                sc.wait_ge(S["yc"], 2 * it + 4)
                sc.dma_start(rows_q[bass.ds(it, 1), :, :].rearrange("o t n -> t (o n)"), ysb).then_inc(S["yo"], 16)

        @block.vector
        def _(ve):
            chain = [0, S["chain"]]
            L = lambda ins: link(ve, chain, ins)
            tt, ts, stt, cp = ve.tensor_tensor, ve.tensor_scalar, ve.scalar_tensor_tensor, ve.tensor_copy
            M, A_, SUB = ALU.mult, ALU.add, ALU.subtract
            bc = lambda v, n, inner: v.unsqueeze(2).broadcast_to([P, n, inner])
            hv = lambda v: v.rearrange("p (h k) -> p h k", k=HD)

            ve.sem_inc(S["actd"], 2)
            ve.wait_ge(S["condq"], 1)
            cp(condf[:, 0, :], B[7][:, 0:16]).then_inc(S["condq"], 1)
            ve.wait_ge(S["condq"], 3)
            L(stt(condf[:, 1, :], condf[:, 1, :], 1.0, condf[:, 0, :], A_, M))
            ts(condT[:, :, :].rearrange("p k i -> p i k"), condf[:, 1, :].rearrange("p (i k) -> p i k", i=2),
               0.5, None, M).then_inc(S["condq"], 1)

            for j in range(NT):
                ve.wait_ge(s_xl[j], 16)
                L(ve.tensor_tensor_reduce(junk, xb[:, j, :], xb[:, j, :], 1.0, 0.0, M, A_, stat[:, j:j + 1]))
                ts(stat[:, 4 + j:5 + j], stat[:, j:j + 1], 1.0 / D, EPS, M, A_).then_inc(S["ssq"], 1)

            def modulation(m):
                if m == 0:
                    ve.wait_ge(S["bada"], 16)
                ve.wait_ge(S["wdone"], turn["ada", m] + 1)
                seg = modrow[:, m * CH:(m + 1) * CH]
                tt(seg, B[6 + m % 2][0:2, :], seg, A_).then_inc(S["modrow"], 1)

            for m in range(ADA1):
                modulation(m)
            ve.wait_ge(S["n1"], 16)
            ve.wait_ge(S["modb1"], 64)
            for i in range(2):
                L(stt(scb[:, i, :], scb[:, i, :], 1.0, nrm, A_, M))
            for j in range(NT):
                i = min(j, 1)
                ve.wait_ge(S["rstd"], j + 1)
                L(stt(xb[:, j, :], xb[:, j, :], stat[:, 8 + j:9 + j], scb[:, i, :], M, M))
                tt(xb[:, j, :], xb[:, j, :], shb[:, i, :], A_).then_inc(S["htok"], 1)
            for j in range(NT):
                ve.wait_ge(S["htr"], 2 * j + 2)
                cp(hT[:, 4:8, j * P:(j + 1) * P], B[2 * (j % 2) + 1].rearrange("p (k t) -> p k t", k=4))\
                    .then_inc(S["hTv"], 1)
            for i, (m, j) in enumerate(zunits):
                if m < NZ and i % 2:
                    c, n = ZCHUNKS[m]
                    z_multiplied(ve, i)
                    cp(zbuf[:, j, c:c + n], B[i % 6][:, 0:n]).then_inc(S["zV"], 1)
            z_evacuated(ve, NZ * NT - 2)
            z_evacuated(ve, NZ * NT - 1)

            ve.wait_ge(S["cons2"], 16 * NCONS2)
            ve.wait_ge(S["cons3"], 16 * NCONS3)
            for j in range(NT):
                zq = zbuf[:, j, ZQ:ZQ + NQK * HD].rearrange("p (h k) -> p h k", k=HD)
                sqv = sq.rearrange("p (h k) -> p h k", k=HD)
                L(tt(sqv, zq, zq, M))
                L(ve.tensor_reduce(stat[:, 16:26], sqv, X, A_))
                ts(stat[:, 26:36], stat[:, 16:26], 1.0 / HD, EPS, M, A_).then_inc(S["anorm"], 1)
                ve.wait_ge(S["arstd"], j + 1)
                L(tt(qk[:, j, :, :], zq, bc(stat[:, 36:46], NQK, HD), M))
                L(tt(qk[:, j, 0:NHQ, :], qk[:, j, 0:NHQ, :], gqk[:, 0:1, :].broadcast_to([P, NHQ, HD]), M))
                ins = tt(qk[:, j, NHQ:NQK, :], qk[:, j, NHQ:NQK, :], gqk[:, 1:2, :].broadcast_to([P, NKV, HD]), M)
                if j == 0:
                    ins.then_inc(S["aqk"], 1)
                    continue
                L(ins)
                v5 = qk[:, j, :, :].rearrange("p h (a s i) -> p h a s i", a=2, s=2)
                x1_, x2_ = v5[:, :, :, 0, :], v5[:, :, :, 1, :]
                cs = [rope[:, j - 1:j, t, :, :].broadcast_to([P, NQK, 2, 16]) for t in range(2)]
                r4 = [rt[:, t, :].rearrange("p (h a i) -> p h a i", h=NQK, a=2) for t in range(4)]
                L(tt(r4[0], x1_, cs[0], M))
                L(tt(r4[1], x2_, cs[1], M))
                L(tt(r4[2], x2_, cs[0], M))
                L(tt(r4[3], x1_, cs[1], M))
                L(tt(x1_, r4[0], r4[1], SUB))
                tt(x2_, r4[2], r4[3], A_).then_inc(S["aqk"], 1)
            for m in range(ADA1, ADA):
                modulation(m)
            ve.wait_ge(S["cachekv"], 32)
            for j in range(NT + 1):
                src = qk[:, j, NHQ:NQK, :] if j < NT else ckv[:, 0, :].rearrange("p (g k) -> p g k", g=NKV)
                ve.wait_ge(S["aqk"], min(j + 1, NT))
                for g in range(NKV):
                    ins = cp(kdup[:, 2 * g:2 * g + 2, :], src[:, g:g + 1, :].broadcast_to([P, 2, HD]))
                ins.then_inc(S["kdupd"], 1)
                ve.wait_ge(S["ktr"], j + 1)
                cp(KT[:, :, j * P:(j + 1) * P], B[1][:, 0:2 * P].rearrange("p (g t) -> p g t", g=NKV))\
                    .then_inc(S["kTv"], 1)

            def row_max(n):
                nk = P if aunits[n][0] == 0 else 3 * P
                ve.wait_ge(S["smm"], n + 1)
                if n >= 2:
                    ve.wait_ge(S["prob"], n - 1)
                L(ve.tensor_reduce(stat[:, 48 + n % 2:49 + n % 2], B[2 + n % 2][:, 0:nk], X, ALU.max))
                ts(stat[:, 50 + n % 2:51 + n % 2], stat[:, 48 + n % 2:49 + n % 2], -SCALE, None, M).then_inc(S["nmax"], 1)

            def probs_back(n):
                nk = P if aunits[n][0] == 0 else 3 * P
                ve.wait_ge(S["prob"], n + 1)
                if n >= 2:
                    ve.wait_ge(S["ya"], n - 1)
                ve.reciprocal(stat[:, 54 + n % 2:55 + n % 2], stat[:, 52 + n % 2:53 + n % 2]).then_inc(S["rinv"], 1)
                ve.wait_ge(S["ptr"], n + 1)
                cp(probT[:, n % 2, 0:nk], B[4 + n % 2][:, 0:nk]).then_inc(S["ptc"], 1)

            for n in range(len(aunits) + 1):
                if n < len(aunits):
                    row_max(n)
                if n >= 1:
                    probs_back(n - 1)

            ve.wait_ge(S["tg"], 2)
            ts(zbuf[:, :, ZGD:ZGD + P], zbuf[:, :, ZGD:ZGD + P], 0.5, 0.5, M, A_).then_inc(S["sgd"], 1)
            ve.wait_ge(S["zfill"], 16 * NEXTRA)
            for j in range(NT):
                kj = kkn[:, j, :]
                L(tt(kj, zbuf[:, j, ZK:ZK + DR], kkb, M))
                L(tt(sq[:, 0:DR], kj, kj, M))
                L(ve.tensor_reduce(stat[:, 0:8], hv(sq[:, 0:DR]), X, A_))
                ts(stat[:, 8:16], stat[:, 0:8], KK_EPS, None, A_).then_inc(S["kkss"], 1)
                ve.wait_ge(S["kkr"], j + 1)
                tt(hv(kj), hv(kj), bc(stat[:, 16:24], HR, HD), M).then_inc(S["kkd"], 1)
            ve.wait_ge(S["ttr"], 2)
            cp(adT, B[1][:, 0:NT * P]).then_inc(S["tcV"], 1)
            for d in range(2):
                ve.wait_ge(S["sttr"], d + 1)
                cp(states[:, d, :, :], B[3][:, 0:4 * HD].rearrange("p (c v) -> p c v", c=4)).then_inc(S["stev"], 1)

            ve.wait_ge(S["modd"], 32)
            L(ve.memset(S0P, 0.0))
            touched = set()
            for u, (d, j) in enumerate(units):
                lat = j > 0
                zr, zk = zbuf[:, j, ZR:ZR + DR], zbuf[:, j, ZK:ZK + DR]
                for i, (t, row) in enumerate(((T1, w0b), (T2, a0b))):
                    ve.wait_ge(S["lora"], 2 * u + i + 1)
                    tt(t, B[i], row[:, d, :], A_).then_inc(S["lt1"], 1)
                ve.wait_ge(S["ltanh"], 2 * u + 1)
                ts(LW, T1, -CDEC / 2, -CDEC / 2, M, A_).then_inc(S["lw"], 1)
                ve.wait_ge(S["ltanh"], 2 * u + 2)
                L(ts(AA, T2, 0.5, 0.5, M, A_))
                L(stt(T1, AA, -1.0, kab, A_, M))
                L(stt(KD, T1, 1.0, zk, A_, M))
                L(tt(T2, kkn[:, j, :], AA, M))
                ve.wait_ge(S["lexp"], 4 * u + 2)
                tt(BT_, T2, EN, M).then_inc(S["bkd"], 1)
                tt(KT_, KD, EN, M).then_inc(S["bkd"], 1)
                L(tt(T1, KD, zr, M))
                L(tt(T1, T1, rkb, M))
                L(ve.tensor_reduce(bonus[:, j, d, :], hv(T1), X, A_))
                if lat:
                    ve.wait_ge(S["lexp"], 4 * u + 4)
                    for i in range(2):
                        r = slice(i * HD, (i + 1) * HD)
                        ins = tt(S0P[r, :, i, :], states[r, d, :, :], ecol[r, :, 0:1].broadcast_to([HD, 4, HD]), M)
                        L(ins) if i == 0 else ins.then_inc(S["s0p"], 1)
                for i, dst in enumerate((BTT, KTT)):
                    ve.wait_ge(S["ttr4"], 4 * u + 3 + i)
                    cp(dst.rearrange("p a b -> p (a b)"), B[5 + i]).then_inc(S["bkT"], 1)
                for h in range(HR):
                    ve.wait_ge(S["gram"], 8 * u + h + 1)
                    tt(AM[:, h, :, :].rearrange("p a b -> p (a b)"), B[gbank[h]], gramm[:, d, :], M).then_inc(S["am"], 1)
                idb = ident[:, :].unsqueeze(1).broadcast_to([P, 4, P])
                b4 = lambda b: B[b].rearrange("p (a b) -> p a b", a=4)
                for g in range(2):
                    ve.wait_ge(s_at[g], 7 * u + 1)
                    ve.wait_ge(s_p[g], 6 * u + 1)
                    tt(XM[g], idb, b4(2 + 3 * g), SUB).then_inc(S["chain"], 1)
                    chain[0] += 1
                    tt(XT[g], idb, ATL[g][0], SUB).then_inc(s_x[g], 1)
                for l in range(1, LEVELS - 1):
                    for g in range(2):
                        ve.wait_ge(s_d[g], 5 * u + l)
                        ve.wait_ge(s_x[g], 6 * u + l)
                        if l < LEVELS - 2:
                            tt(XM[g], XM[g], b4(3 + 3 * g), SUB).then_inc(S["chain"], 1)
                            chain[0] += 1
                        tt(XT[g], XT[g], b4(4 + 3 * g), SUB).then_inc(s_x[g], 1)
                for g in range(2):
                    ve.wait_ge(s_u[g], 4 * u + 4)
                    ve.wait_ge(s_uc[g], 4 * u + 3)
                    tt(UU[g].rearrange("p a b -> p (a b)"), B[2 + 3 * g][:, 0:4 * HD],
                       U1[g].rearrange("p a b -> p (a b)"), SUB).then_inc(s_uc[g], 1)
                for g in range(2):
                    ve.wait_ge(S["yout"], 2 * u + g + 1)
                    dst = yrw[:, j, g * 256:(g + 1) * 256]
                    if (j, g) in touched:
                        ve.wait_ge(S["yrd"], 2 * u + g)
                        tt(dst, B[3 + 3 * g][:, 0:256], dst, A_).then_inc(S["yrd"], 1)
                    else:
                        cp(dst, B[3 + 3 * g][:, 0:256]).then_inc(S["yrd"], 1)
                    touched.add((j, g))
                    if u in LAST:
                        continue
                    ve.wait_ge(S["twod"], st_index[u] + g + 1)
                    t2 = B[4 + 3 * g][:, 0:2 * HD].rearrange("p (c v) -> p c v", c=2)
                    end = ecol[:, 2 * g:2 * g + 2, 1:2].broadcast_to([P, 2, HD])
                    if lat:
                        s = states[:, d, 2 * g:2 * g + 2, :]
                        for i in range(2):
                            r = slice(i * HD, (i + 1) * HD)
                            L(tt(s[r], t2[r], S0P[r, 2 * g:2 * g + 2, i, :], A_))
                        tt(s, s, end, M).then_inc(S["st2"], 1)
                    else:
                        ve.wait_ge(S["lexp"], 4 * u + 4)
                        tt(sfin[:, 2 * g:2 * g + 2, :], t2, end, M).then_inc(S["st2"], 1)
                if u not in LAST:
                    ve.wait_ge(S["st2"], st_index[u] + 2)

            ve.wait_ge(S["yrd"], 2 * NU)
            ve.wait_ge(S["lnld"], 32)
            for j in range(NT):
                L(ve.tensor_reduce(stat[:, 0:8], hv(yrw[:, j, :]), X, A_))
                L(ts(stat[:, 0:8], stat[:, 0:8], 1.0 / HD, None, M))
                if j:
                    ve.wait_ge(S["ytr"], 2 * j - 1)
                L(tt(hv(yc), hv(yrw[:, j, :]), bc(stat[:, 0:8], HR, HD), SUB))
                L(tt(ysq, yc, yc, M))
                L(ve.tensor_reduce(stat[:, 24:32], hv(ysq), X, A_))
                ts(stat[:, 8:16], stat[:, 24:32], 1.0 / HD, GN_EPS, M, A_).then_inc(S["kkss"], 1)
                ve.wait_ge(S["kkr"], NT + j + 1)
                L(tt(hv(yc), hv(yc), bc(stat[:, 16:24], HR, HD), M))
                L(tt(yc, yc, lnw, M))
                L(tt(yc, yc, lnb, A_))
                L(tt(stat[:, 24:32], bonus[:, j, 0, :], bonus[:, j, 1, :], A_))
                L(tt(hv(ysq), hv(zbuf[:, j, ZV:ZV + DR]), bc(stat[:, 24:32], HR, HD), M))
                L(tt(yc, yc, ysq, A_))
                ve.wait_ge(S["gps"], j + 1)
                tt(yc, B[6], yc, M).then_inc(S["yfin"], 1)
                ve.wait_ge(S["upm"], j + 1)
                ve.wait_ge(S["gld"], 16 * (j + 1))
                if j:
                    ve.wait_ge(S["mtr"], 2 * j)
                for i, dst in enumerate((mg, mg2)):
                    for n in range(2):
                        L(stt(dst[:, n * CH:(n + 1) * CH], gld[:, i * D + n * CH:i * D + (n + 1) * CH], 1.0,
                              B[2 * i + n], A_, M))
                tt(mg, mg, mg2, A_).then_inc(S["mrg"], 1)
            for j in range(NT):
                ve.wait_ge(S["xr"], 16 * (j + 1))
                ve.wait_ge(S["g1l"], 16 * (1 + min(j, 1)))
                for n in range(2):
                    ve.wait_ge(S["wout"], 2 * j + n + 1)
                    seg = slice(n * CH, (n + 1) * CH)
                    L(tt(x1[:, j, seg], B[2 * (j % 2) + n], g1b[:, seg], M))
                    ins = tt(x1[:, j, seg], x1[:, j, seg], xr2[:, seg], A_)
                    if n == 0:
                        L(ins)
                    else:
                        ins.then_inc(S["x1s"], 1)
            ve.wait_ge(S["x1s"], NT)
            for j in range(NT):
                L(ve.tensor_tensor_reduce(jk, x1[:, j, :], x1[:, j, :], 1.0, 0.0, M, A_, stat[:, j:j + 1]))
                ts(stat[:, 4 + j:5 + j], stat[:, j:j + 1], 1.0 / D, EPS, M, A_).then_inc(S["ssq"], 1)
            ve.wait_ge(S["n1"], 32)
            for j in range(NT):
                if j < 2:
                    ve.wait_ge(S["n2l"], 32 * (j + 1))
                    L(stt(sc2, sc2, 1.0, n2, A_, M))
                ve.wait_ge(S["rstd"], NT + j + 1)
                if j:
                    ve.wait_ge(S["h2out"], 16 * j)
                    ve.wait_ge(S["h2tr"], 2 * j)
                L(stt(h2, x1[:, j, :], stat[:, 8 + j:9 + j], sc2, M, M))
                tt(h2, h2, sh2, A_).then_inc(S["h2s"], 1)

            ve.wait_ge(S["lg"], NT)
            ve.wait_ge(S["cons4"], 16 * NCONS4)
            lv = lgt[:, :, :]
            L(tt(lv, B[6][:, 0:NT * NE].rearrange("p (j e) -> p j e", j=NT),
                 brow.unsqueeze(1).broadcast_to([P, NT, NE]), A_))
            for j in range(NT):
                L(ve.max(mx8[:, j, :], lgt[:, j, :]))
                L(ve.max_index(ix8[:, j, :], mx8[:, j, :], lgt[:, j, :]))
            tt(exd, mx8[:, :, 0:TOPK], mx8[:, :, 0:1].broadcast_to([P, NT, TOPK]), SUB).then_inc(S["exa"], 1)
            L(cp(ixf.rearrange("p (j k) -> p j k", j=NT), ix8[:, :, 0:TOPK]))
            L(tt(onehot, iota[:, 0:NE].unsqueeze(1).broadcast_to([P, 12, NE]),
                 ixf.unsqueeze(2).broadcast_to([P, 12, NE]), ALU.is_equal))
            for j in range(NT):
                ins = ve.tensor_reduce(selm[:, j, :], onehot[:, 4 * j:4 * j + 4, :].rearrange("p k e -> p e k"), X, A_)
                L(ins) if j < NT - 1 else ins.then_inc(S["routeq"], 1)
            ve.wait_ge(S["exb"], 1)
            L(ve.tensor_reduce(sum3, exd, X, A_))
            L(ve.reciprocal(sum3, sum3))
            L(tt(gate[:, :, :], exd, sum3.unsqueeze(2).broadcast_to([P, NT, TOPK]), M))
            ve.wait_ge(S["routeq"], 3)
            L(cp(rkm, B[7][:, 0:NT * NE].rearrange("p (j e) -> p j e", j=NT)))
            L(tt(acol, B[5][0:QMAX, 0:1], cq[0:QMAX, 2:3], ALU.is_gt))
            cp(aspread, acol.broadcast_to([QMAX, P])).then_inc(S["routeq"], 1)
            ve.wait_ge(S["routeq"], 1)
            L(stt(rsel, rkm, 1000.0, selm, A_, M))
            for q in range(NB):
                L(ts(rankm[:, :, q * NE:(q + 1) * NE], rsel, -1000.0 - P * q, None, A_))
            ve.wait_ge(S["routeq"], 5)
            L(cp(pcol, B[4][0:QMAX, 0:1]))
            L(cp(posb, B[4][:, P:P + QMAX]))
            ts(lsto, iota[0:QMAX, :], pcol, acol, ALU.is_equal, M).then_inc(S["routeq"], 1)
            for j in range(NT):
                ins = ts(cmp[:, j, :], iota, rankm[:, j, 0:1], None, ALU.is_equal)
            ins.then_inc(S["cmpd"], 1)
            ve.wait_ge(S["routeq"], 7)
            cp(tab[:, :], B[3][0:1, 0:2 * P + 1]).then_inc(S["routeq"], 1)
            for j in range(NT):
                L(tt(ohr[:, 4 * j:4 * j + 4, :], onehot[:, 4 * j:4 * j + 4, :],
                     rkm[:, j:j + 1, :].broadcast_to([P, 4, NE]), M))
            L(ve.tensor_reduce(rkf, ohr, X, A_))
            L(tt(pdif, posb[:, NE:QMAX], posb[:, 0:QMAX - NE], SUB))
            for i in range(2):
                L(tt(ohr, onehot, pdif[:, i * NE:(i + 1) * NE].unsqueeze(1).broadcast_to([P, 12, NE]), M))
                L(ve.tensor_reduce(d12[i], ohr, X, A_))
                L(ts(d12[i], d12[i], -1.0, float(P), A_, M))
            L(stt(ixf, ixf, float(P), rkf, M, A_))
            for i in range(2):
                L(stt(s12, rkf, float(P * (i + 1)), d12[i], ALU.is_ge, M))
                ins = tt(ixf if i == 0 else dest[:, :], ixf, s12, A_)
                L(ins)
            ve.wait_ge(S["b32"], 16 * 2 * NB)
            for c in range(6):
                seg = slice(c * CH, (c + 1) * CH)
                src = bias32[0:QMAX, seg]
                L(cp(btb[0:QMAX, :], src))
                L(cp(b3[0:NE, seg], btb[0:NE, :]))
                L(tt(bt0[0:QMAX, :], src, btb[0:QMAX, :], SUB))
                L(cp(btb[0:QMAX, :], bt0[0:QMAX, :]))
                L(cp(b3[NE:2 * NE, seg], btb[NE:2 * NE, :]))
                L(tt(bt1[0:QMAX, :], bt0[0:QMAX, :], btb[0:QMAX, :], SUB))
                ins = cp(b3[2 * NE:QMAX, seg], bt1[2 * NE:QMAX, :])
                L(ins) if c < 5 else ins.then_inc(S["b3d"], 1)

            nblk = ve.value_load(tab[0:1, 2 * P:2 * P + 1], min_val=NE, max_val=NBMAX)
            with ve.Fori(0, nblk) as it:
                q = ve.value_load(tab[0:1, bass.ds(it + 1, 1)], min_val=0, max_val=QMAX - 1)
                lchain = [0, S["chain2v"]]
                PER = 4
                LL = lambda ins: link(ve, lchain, ins, PER * it)
                ve.wait_ge(S["idxm"], it + 1)
                for j in range(NT):
                    ins = ts(cmp[:, j, :], iota, rankm[:, j, bass.ds(q, 1)], None, ALU.is_equal)
                ins.then_inc(S["cmpd"], 1)
                for h in range(2):
                    ve.wait_ge(S["hmm"], 4 * it + (2 * h + 1))
                    ts(gl, B[2 * h], LIMIT, None, ALU.min).then_inc(S["gld2"], 1)
                    ve.wait_ge(S["hmm"], 4 * it + (2 * h + 2))
                    ve.wait_ge(S["actd"], 2 * it + (h + 2))
                    LL(ts(uu, B[2 * h + 1], LIMIT, -LIMIT, ALU.min, ALU.max))
                    ve.wait_ge(S["gld2"], 2 * it + (h + 1))
                    LL(stt(uu, uu, 1.0, gl, A_, M))
                    ve.wait_ge(S["thd"], 2 * it + (h + 1))
                    stt(act[:, h * CH:(h + 1) * CH], th, 1.0, uu, A_, M).then_inc(S["actd"], 1)
                assert lchain[0] == PER
                ve.wait_ge(S["ymm"], it + 1)
                ve.wait_ge(S["yo"], 16 * it + 16)
                cp(ysb[:, 0:CH], B[4]).then_inc(S["yc"], 1)

            ve.wait_ge(S["fld"], 48)
            for j in range(NT):
                for k in range(TOPK):
                    n = TOPK * j + k
                    ve.wait_ge(s_yg[n % 4], 16 * (n // 4 + 1))
                    w = gate[:, j, k:k + 1]
                    if k == 0:
                        if j:
                            ve.wait_ge(S["fin"], j)
                        ins = ts(facc, ygat[n % 4], w, None, M)
                    else:
                        ve.wait_ge(S["ygc"], n)
                        ins = stt(facc, ygat[n % 4], w, facc, M, A_)
                    ins.then_inc(S["ygc"], 1)
                ve.wait_ge(S["ygc"], TOPK * (j + 1))
                L(tt(facc, facc, g2b[min(j, 1)], M))
                L(tt(facc, facc, x1[:, j, :], A_))
                L(ve.tensor_tensor_reduce(jk, facc, facc, 1.0, 0.0, M, A_, stat[:, j:j + 1]))
                ts(stat[:, 4 + j:5 + j], stat[:, j:j + 1], 1.0 / D, EPS, M, A_).then_inc(S["ssq"], 1)
                ve.wait_ge(S["rstd"], 2 * NT + j + 1)
                stt(x1[:, j, :], facc, stat[:, 8 + j:9 + j], nfb, M, M).then_inc(S["fin"], 1)


_INS = ["x_prompt", "x_sample", "cache_k", "cache_v", "state_rwkv_fwd", "state_rwkv_bwd", "c", "c_ctx", "w_ada",
        "b_ada", "norm1", "norm2", "w_in", "rw_w0", "rw_w2", "rw_a0", "rw_a2", "rw_g2", "rw_kk", "rw_ka", "rw_rk",
        "rw_ln_w", "rw_ln_b", "q_norm", "k_norm", "w_up_r", "w_up_a", "w_out", "w_router", "b_router",
        "w_moe_in", "b_moe_in", "w_moe_out", "b_moe_out", "norm_f"]
_OUTS = [("y_prompt", (1, P, D)), ("y_sample", (1, 2 * P, D)), ("new_cache_k", (1, 1, P, NKV, HD)),
         ("new_cache_v", (1, 1, P, NKV, HD)), ("new_state_fwd", (1, 1, HR, HD, HD)),
         ("new_state_bwd", (1, 1, HR, HD, HD))]


def kernel(**inputs):
    import concourse.bacc as bacc
    from concourse.bass_utils import run_bass_kernel_spmd

    nc = bacc.Bacc("TRN2", target_bir_lowering=False, num_devices=1, dynamic_dma_scratch_size=8192)
    arrays, a, o = {}, {}, {}
    for name in _INS:
        arrays[name] = np.ascontiguousarray(inputs[name])
    arrays.update(_CONST)
    for name, v in arrays.items():
        a[name] = nc.dram_tensor(name, v.shape, mybir.dt.from_np(v.dtype), kind="ExternalInput").ap()
    for name, shape in _OUTS:
        o[name] = nc.dram_tensor(name, shape, F32, kind="ExternalOutput").ap()
    build(nc, a, o)
    r = run_bass_kernel_spmd(nc, [arrays], core_ids=[0])
    return tuple(r.results[0][name] for name, _ in _OUTS)
```

```python
from contextlib import ExitStack

import concourse.bass as bass
from concourse import mybir
import numpy as np

F32 = mybir.dt.float32
BF16 = mybir.dt.bfloat16
F32R = mybir.dt.float32r
I32 = mybir.dt.int32
U32 = mybir.dt.uint32
U16 = mybir.dt.uint16
ALU = mybir.AluOpType
ACT = mybir.ActivationFunctionType
X = mybir.AxisListType.X

P = 128
D = 1024
KC = D // P
NT = 3
DR = 512
HR = 8
HD = 64
RANK = 64
NHQ = 8
NKV = 2
NE = 32
TOPK = 4
FF = 1024
PAST = 128
EPS = 1e-6
GN_EPS = 64e-5
KK_EPS = 1e-12
ALPHA = 1.702
LIMIT = 7.0
CDEC = float(np.exp(-0.5))
SCALE = HD ** -0.5

ZR, ZK, ZV, ZWD, ZAD, ZGD, ZQ = 0, 512, 1024, 1536, 1664, 1792, 1920
ZKA, ZVA, ZW = 2432, 2560, 2688
CH = 512
ZCHUNKS = [(c, min(CH, ZW - c)) for c in range(0, ZW, CH)]
GCHUNKS = [(ZW + c, CH) for c in range(0, 2 * D, CH)]
NZ = len(ZCHUNKS)
ADA = 6 * D // CH
ADA1 = 4
ADA2 = ADA1 + 2
NQK = NHQ + NKV
ZQC = 4
KQ = KC // ZQC
ZQ_ALL = ZQC * (NZ + 2 * D // CH)
LEVELS = 7
NB = 3
QMAX = NE * NB
NEXTRA = NT * P * TOPK // (P + 1)
NBMAX = NE + NEXTRA
SLOT = KC * CH
CW = SLOT // 2
W1C = 2 * FF // CH * 2
W2C = D * FF // P // CW
WC = W1C + W2C
NRAW, NPAIR = 6, 4
POOL_LO = (1, 5, 9)


def constants():
    s = np.arange(P)[:, None]
    t = np.arange(P)[None, :]
    out = {}
    mid = P // 2 - 1
    inc_f = (s <= t).astype(np.float32) - (s <= mid)
    exc_f = (s < t).astype(np.float32) - (s <= mid)
    inc_b = (s >= t).astype(np.float32) - (s > mid)
    exc_b = (s > t).astype(np.float32) - (s > mid)
    out["c_ident"] = np.eye(P, dtype=np.float32)
    out["c_cum"] = np.stack([inc_f, exc_f, inc_b, exc_b], 1).reshape(P, 4 * P).astype(np.float32)
    first = np.arange(P) <= mid
    col = np.stack([first, ~first, ~first, first], 1).astype(np.float32)
    out["c_col"] = col
    gram = []
    for d in range(2):
        strict = (s < t) if d == 0 else (s > t)
        incl = (s <= t) if d == 0 else (s >= t)
        gram.append(np.concatenate([strict, incl, strict, incl], 1))
    out["c_gram"] = np.concatenate(gram, 1).astype(np.uint16) * np.uint16(0x3F80)
    lev = []
    for d in range(2):
        for l in range(LEVELS):
            same = (s >> (l + 1)) == (t >> (l + 1))
            sb, tb = (s >> l) & 1, (t >> l) & 1
            lev.append(same & ((sb == 0) & (tb == 1) if d == 0 else (sb == 1) & (tb == 0)))
    out["c_level"] = np.concatenate(lev, 1).astype(np.uint16) * np.uint16(0x3F80)
    inv = 10000.0 ** (-np.arange(0, HD // 2, 2, dtype=np.float32) / np.float32(HD // 2))
    pos = np.arange(2 * P)
    row, colp = (pos // 64).astype(np.float32), (pos % 64).astype(np.float32)
    ang = np.stack([row[:, None] * inv[None], colp[:, None] * inv[None]], 1).astype(np.float32)
    cs = np.stack([np.cos(ang), np.sin(ang)], 1).astype(np.float32)
    out["c_rope"] = cs.reshape(2, P, 64).transpose(1, 0, 2).reshape(P, 128).copy()
    out["c_rank"] = np.concatenate([(s < t), np.ones((P, P))], 1).astype(np.float32)
    out["c_tok"] = (np.arange(P)[:, None] + P * np.arange(NT)[None]).astype(np.float32)
    out["c_iota"] = np.broadcast_to(np.arange(P, dtype=np.float32), (P, P)).copy()
    q = np.arange(P)
    thr = np.where(q < NE, -1.0, np.where(q < 2 * NE, P, 2 * P)).astype(np.float32)
    out["c_q"] = np.stack([q, q % NE, thr, np.ones(P)], 1).astype(np.float32)
    sel = np.zeros((QMAX, NE, P), np.uint16)
    for e in range(NE):
        sel[e::NE, e, :] = 0x3F80
    out["c_sel"] = sel.reshape(QMAX, NE * P)
    return out


_CONST = constants()


def build(nc, a, o):
    ctx = ExitStack()
    with ctx:
        sb = lambda n, s, d=F32: ctx.enter_context(nc.sbuf_tensor(n, s, d))
        sem = lambda n: ctx.enter_context(nc.semaphore(n))
        dram = lambda n, s: nc.dram_tensor(n, s, F32, kind="Internal").ap()

        mods_d = dram("mods_d", (2, 6 * D))
        gates_d = dram("gates_d", (NT, P, 2 * D))
        h2_d = dram("h2_d", (NT * P, D))
        rows_d = dram("rows_d", (NBMAX * P, D))

        ring = sb("ring", [P, 3 * SLOT])
        zbuf = sb("zbuf", [P, NT, ZW])
        ky = sb("ky", [P, 2 * NT * DR])
        rowc = sb("rowc", [P, 7 * DR])
        smallw = sb("smallw", [P, 3 * DR + KC * NE])
        turned = sb("turned", [P, 3, NT * P])
        ident = sb("ident", [P, P])
        cum = sb("cum", [P, 4, P])
        colm = sb("colm", [P, 4])
        gram16 = sb("gram16", [P, 2 * 4 * P], U16)
        level16 = sb("level16", [P, 2 * LEVELS * P], U16)
        gramm = gram16[:, :].bitcast(BF16).rearrange("p (d n) -> p d n", d=2)
        levelm = level16[:, :].bitcast(BF16).rearrange("p (l n) -> p l n", n=P)
        rope = sb("rope", [P, 2, 2, 2, 16])
        condc = sb("condc", [16, P])
        condf = sb("condf", [P, 2, 16])
        condT = sb("condT", [P, KC, 2])
        stat = sb("stat", [P, 64])
        half = sb("half", [P, 16])
        bonus = sb("bonus", [P, NT, 2, HR])
        states = sb("states", [P, 2, 4, HD])
        sfin = sb("sfin", [P, 4, HD])
        stout = sb("stout", [HD, 4 * P])
        tab = sb("tab", [1, 2 * P + 2], I32)
        slots = sb("slots", [P, 1], U32)
        dest = sb("dest", [P, NT * TOPK], U32)
        gate = sb("gate", [P, NT, TOPK])
        with nc.sbuf_tensor("work", [P, 20480], F32) as work:
            pass
        parts = sb("parts", [P, 20480], F32R)

        def at(buf, start, *shape, rows=P):
            n = int(np.prod(shape))
            v = buf[0:rows, start:start + n]
            if len(shape) == 1:
                return v
            names = "abcd"[:len(shape)]
            return v.rearrange(f"p ({' '.join(names)}) -> p {' '.join(names)}",
                               **{names[i]: shape[i] for i in range(len(shape))})

        ring_slot = [at(ring, i * SLOT, KC, CH) for i in range(3)]
        kkn = at(ky, 0, NT, DR)
        yrw = at(ky, NT * DR, NT, DR)
        w0b, a0b = at(rowc, 0, 2, DR), at(rowc, 2 * DR, 2, DR)
        kkb, kab, rkb = (at(rowc, i * DR, DR) for i in (4, 5, 6))
        w2s, a2s, g2s = (at(smallw, i * DR, DR) for i in (0, 1, 2))
        wrout = at(smallw, 3 * DR, KC, NE)
        twT, adT, sgT = turned[:, 0, :], turned[:, 1, :], turned[:, 2, :]
        modrow = at(work, 3072, 6 * D, rows=2)
        nrm = at(work, 9216, D)
        scb, shb = at(work, 10240, 2, D), at(work, 12288, 2, D)
        xb = at(work, 14336, NT, D)
        junk = at(work, 17408, D)
        gst = at(work, 18432, 4, CH)
        QT, KT = at(work, 0, 4, NT * P), at(work, 1536, 2, 4 * P)
        qk = at(work, 9216, NT, NQK, HD)
        rt = at(work, 11136, 4, NQK * 32)
        gqk = at(work, 12416, 2, HD)
        kdup = at(work, 13056, 4, HD)
        ckv = at(work, 13312, 2, NKV * HD)
        prob = at(work, 13568, 2, 3 * P)
        probT = at(work, 14336, 2, 3 * P)
        sq = at(work, 15104, NQK * HD)
        LW, AA, T1, T2 = (at(work, i * DR, DR) for i in range(4))
        ER, EQ, EN = (at(work, 2048 + i * DR, DR) for i in range(3))
        RQ = at(work, 3584, 2, DR)
        BT_, KT_ = at(work, 4608, DR), at(work, 5120, DR)
        KD = at(work, 5632, DR)
        QRT = at(work, 6144, 4, 2, P)
        BTT, KTT = at(work, 7168, 4, P), at(work, 7680, 4, P)
        AM = at(work, 8192, HR, 4, P)
        ATL = [[at(work, 12288 + (2 * g + b) * DR, 4, P) for b in range(2)] for g in range(2)]
        XM = [at(work, 14336 + g * 3 * DR, 4, P) for g in range(2)]
        XT = [at(work, 14848 + g * 3 * DR, 4, P) for g in range(2)]
        PM = [at(work, 15360 + g * 3 * DR, 4, P) for g in range(2)]
        GM, U1, U2, UU = ([at(work, 17408 + g * 1024 + i * 256, 4, HD) for g in range(2)] for i in range(4))
        S0P = at(work, 19456, 4, 2, HD)
        stin = [at(work, i, 4 * P, rows=HD) for i in (19712, 16384)]
        ecol = at(work, 20224, 4, 2)
        yrT, yaT = at(work, 0, 4, NT * P), at(work, 1536, 4, NT * P)
        gld = at(work, 3072, 2 * D)
        mg, mg2 = at(work, 5120, D), at(work, 6144, D)
        mT = at(work, 7168, KC, NT * P)
        lnw, lnb = at(work, 10240, DR), at(work, 10752, DR)
        yc, ysq = at(work, 11264, DR), at(work, 11776, DR)
        x1 = at(ky, 0, NT, D)
        xr2 = at(work, 12288, D)
        g1b = at(work, 13312, D)
        n2 = at(work, 14336, D)
        sc2 = at(work, 15360, D)
        sh2 = at(work, 16384, D)
        h2 = at(work, 17408, D)
        h2T = at(work, 18432, KC, P)
        hTp = [at(parts, i, KC, NT * P) for i in (0, 9216)]
        zpart = lambda t, i, n: at(parts, 13568 + (2 * (t % 2) + i) * KQ * CH, KQ, n)
        raw = lambda c: at(ring, (c + 4) % NRAW * CW, CW)
        part = lambda c, i: at(parts, (2 * (c % NPAIR) + i) * CW, CW)
        xTp, actTp = ([at(parts, (2 * NPAIR) * CW + (2 * q + i) * D, KC, P) for i in range(2)] for q in range(2))
        jk = zbuf[:, :, :].rearrange("p a b -> p (a b)")[:, 5120:6144]
        zf = zbuf[:, :, :].rearrange("p a b -> p (a b)")
        xg, act, ysb = zf[:, 0:1024], zf[:, 1024:2048], zf[:, 2048:3072]
        gl, th, uu = zf[:, 5120:5632], zf[:, 5632:6144], zf[:, 6144:6656]
        cmp = zf[:, 6656:7040].rearrange("p (j t) -> p j t", j=NT)
        rankm = zf[:, 7040:7328].rearrange("p (j q) -> p j q", j=NT)
        crank, iota = zf[:, 7328:7584], zf[:, 7584:7712]
        ctok, cq = zf[:, 7712:7715], zf[:, 7716:7720]
        brow = zf[:, 7720:7752]
        selm = zf[:, 7752:7848].rearrange("p (j e) -> p j e", j=NT)
        lgt = zf[:, 7848:7944].rearrange("p (j e) -> p j e", j=NT)
        mx8 = zf[:, 4096:4120].rearrange("p (j k) -> p j k", j=NT)
        ix8 = zf[:, 4120:4144].bitcast(U32).rearrange("p (j k) -> p j k", j=NT)
        ixf, rkf = zf[:, 4144:4156], zf[:, 4156:4168]
        pcol, acol, s12 = zf[0:QMAX, 4168:4169], zf[0:QMAX, 4169:4170], zf[:, 4170:4182]
        exd = zf[:, 4182:4194].rearrange("p (j k) -> p j k", j=NT)
        sum3 = zf[:, 4194:4197]
        rkm = zf[:, 4224:4320].rearrange("p (j e) -> p j e", j=NT)
        rsel = zf[:, 4320:4416].rearrange("p (j e) -> p j e", j=NT)
        aspread, posb = zf[0:QMAX, 5376:5504], zf[:, 5504:5600]
        pdif, d12 = zf[:, 5600:5664], [zf[:, 5664:5676], zf[:, 5676:5688]]
        lsto = zf[0:QMAX, 4416:4544]
        onehot = zf[:, 4608:4992].rearrange("p (k e) -> p k e", e=NE)
        ohr = zf[:, 4992:5376].rearrange("p (k e) -> p k e", e=NE)
        b3 = at(rowc, 0, 1536).bitcast(BF16)
        selc = at(rowc, 1536, 2048).bitcast(BF16).rearrange("p (e t) -> p e t", e=NE)
        bias32 = at(work, 16384, 3072)
        ygat = [at(work, i * D, D) for i in range(NT * TOPK)]
        facc, nfb = zf[:, 0:1024], at(smallw, 0, D)
        g2b = [zf[:, 3072:4096], zf[:, 4096:5120]]

        pb = [ctx.enter_context(nc.psum_tensor(f"bank{i}", [P, 512], F32)) for i in range(8)]
        B = [b[:, :] for b in pb]

        names = """cond bada n1 modd modb1 ssq rstd htok htr hTa hTv wdone zmm zA zV cons2 cons3
        cachekv nkv anorm arstd aqk kdupd qtr ktr qTa kTv smm nmax prob rinv ptr ptc pv ya tg sgd ttr tcA
        tcV kkss kkr kkd stld sttr stev lora lt1 ltanh lw lcum lexp rqd bkd ttr4 rqT bkT s0p gram am yout
        yrd twod st2 sftr sfcp sfout lnld gld gps yfin ytr yTc upm mrg mtr mTc wout g1l x1s n2l h2s
        h2out h2tr h2Tc lg exa exb b32 b3d selld cmpd idxm idxc xgd xtm xtc mult hi gld2 thd actd atm atc
        xtl atl ymm yc yo fin fout fld chain chain2 gpn zfill chain2v modrow condq routeq""".split()
        S = {n: sem("s_" + n) for n in names}
        s_wld = [sem(f"s_wld{i}") for i in range(3)]
        s_yg = [sem(f"s_yg{j}") for j in range(NT)]
        s_xl = [sem(f"s_xl{j}") for j in range(NT)]
        s_gst = [sem(f"s_gst{i}") for i in range(4)]
        s_at = [sem(f"s_at{g}") for g in range(2)]
        s_p = [sem(f"s_p{g}") for g in range(2)]
        s_pc = [sem(f"s_pc{g}") for g in range(2)]
        s_d = [sem(f"s_d{g}") for g in range(2)]
        s_x = [sem(f"s_x{g}") for g in range(2)]
        s_u = [sem(f"s_u{g}") for g in range(2)]
        s_uc = [sem(f"s_uc{g}") for g in range(2)]
        s_es = [sem(f"s_es{i}") for i in range(NRAW)]
        s_lo = [sem(f"s_lo{i}") for i in range(NPAIR)]

        stream = [("ada", m) for m in range(ADA1)] + [("in", m) for m in range(NZ + 4)]
        stream += [("ada", m) for m in range(ADA1, ADA)] + [("upr", 0), ("upa", 0), ("out", 0), ("out", 1)]
        turn = {k: i for i, k in enumerate(stream)}

        def landed(eng, key):
            i = turn[key]
            eng.wait_ge(s_wld[i % 3], 16 * (i // 3 + 1))

        zunits = [(m, j) for m in range(NZ + 4) for j in range(NT)]

        def z_evacuated(eng, i):
            n = NZ * NT
            if i >= n:
                eng.wait_ge(S["zA"], n // 2 + i - n + 1)
            elif i % 2 == 0:
                eng.wait_ge(S["zA"], i // 2 + 1)
            else:
                eng.wait_ge(S["zV"], i // 2 + 1)

        aunits = [(j, h) for j in range(NT) for h in range(NHQ)]
        units = [(0, 0), (1, 2), (0, 1), (1, 1), (0, 2), (1, 0)]
        NU = len(units)
        CTX = [0, 5]
        LAT = [2, 1]

        LAST = [4, 3]
        lat_index = [sum(units[v][1] > 0 for v in range(u)) for u in range(NU)]
        st_index = [2 * sum(v not in LAST for v in range(u)) for u in range(NU)]
        ada_bank = lambda m: B[6 + m % 2] if m < ADA2 else B[m % 2]
        gbank = [0, 1, 7, 2, 3, 4, 5, 6]

        def z_multiplied(eng, i):
            m, j = zunits[i]
            if j == NT - 1:
                eng.wait_ge(S["mult"], ZQC * (m + 1))
            else:
                eng.wait_ge(S["zmm"], (NT - 1) * m + j + 1)

        def z_order(split):
            for t in range(ZQ_ALL):
                split(t)
                if t % ZQC == 1 and t > ZQC:
                    yield from range(NT * (t // ZQC - 1), NT * (t // ZQC))
            yield from range(len(zunits) - NT, len(zunits))

        def z_quarter(t):
            m, q = t // ZQC, t % ZQC
            return ring_slot[turn["in", m] % 3][:, KQ * q:KQ * q + KQ, 0:(ZCHUNKS + GCHUNKS)[m][1]]

        def z_high(sc, t):
            n = (ZCHUNKS + GCHUNKS)[t // ZQC][1]
            if t % ZQC == 0:
                landed(sc, ("in", t // ZQC))
            if t >= 2:
                sc.wait_ge(S["mult"], t - 1)
            nc.scalar.activation(zpart(t, 0, n), z_quarter(t), ACT.Copy).then_inc(S["hi"], 1)

        def z_low(eng, t):
            n = (ZCHUNKS + GCHUNKS)[t // ZQC][1]
            eng.wait_ge(S["hi"], t + 1)
            eng.tensor_tensor(zpart(t, 1, n), z_quarter(t), zpart(t, 0, n), ALU.subtract)\
               .then_inc(s_lo[t % NPAIR], 1)

        flat = lambda name: a[name].rearrange("o d n -> o (d n)")
        cons2 = [
            (cum[:, :, :].rearrange("p a b -> p (a b)"), a["c_cum"]), (colm[:, :], a["c_col"]),
            (gram16[:, :], a["c_gram"]), (level16[:, :], a["c_level"]),
            (rope[:, :, :, :, :].rearrange("p a b c d -> p (a b c d)"), a["c_rope"]),
            (at(rowc, 0, 2 * DR), flat("rw_w0").broadcast_to([P, 2 * DR])),
            (at(rowc, 2 * DR, 2 * DR), flat("rw_a0").broadcast_to([P, 2 * DR])),
            (kkb, a["rw_kk"].broadcast_to([P, DR])), (kab, a["rw_ka"].broadcast_to([P, DR])),
            (rkb, flat("rw_rk").broadcast_to([P, DR])),
            (w2s, a["rw_w2"].rearrange("o d r n -> (o d r) n")),
            (a2s, a["rw_a2"].rearrange("o d r n -> (o d r) n")),
            (g2s, a["rw_g2"].rearrange("o r n -> (o r) n")),
            (wrout, a["w_router"].rearrange("o (k p) n -> p (o k) n", p=P)),
        ]
        NCONS2, NCONS3, NCONS4 = len(cons2), 2, 5

        def raw_landed(eng, it, c):
            eng.wait_ge(s_es[c % NRAW], 16 * (WC // NRAW * it + (c // NRAW + 1)))

        def low_part_done(eng, it, c):
            eng.wait_ge(s_lo[c % NPAIR], WC // NPAIR * it + (c // NPAIR + 1 + ZQ_ALL // NPAIR))

        def high_part(sc, it, c, free=True):
            raw_landed(sc, it, c)
            if free:
                sc.wait_ge(S["mult"], WC * it + (c - NPAIR + 1 + ZQ_ALL))
            nc.scalar.activation(part(c, 0), raw(c), ACT.Copy).then_inc(S["hi"], 1)

        def low_part(eng, it, c):
            eng.wait_ge(S["hi"], WC * it + (c + 1 + ZQ_ALL))
            eng.tensor_tensor(part(c, 1), raw(c), part(c, 0), ALU.subtract).then_inc(s_lo[c % NPAIR], 1)

        block = ctx.enter_context(nc.Block())

        def link(eng, chain, ins, base=0):
            chain[0] += 1
            ins.then_inc(chain[1], 1)
            eng.wait_ge(chain[1], base + chain[0])

        @block.sync
        def _(sp):
            sp.dma_start(condc[0:8, :], a["c_ctx"].rearrange("(k p) -> k p", p=P)).then_inc(S["cond"], 16)
            sp.dma_start(condc[8:16, :], a["c"].rearrange("o (k p) -> (o k) p", p=P)).then_inc(S["cond"], 16)
            sp.dma_start(ident[:, :], a["c_ident"]).then_inc(S["cond"], 16)
            sp.dma_start(modrow, a["b_ada"].broadcast_to([2, 6 * D])).then_inc(S["bada"], 16)

            def weights(key):
                i = turn[key]
                kind, m = key
                if key == ("out", 1):
                    sp.wait_ge(S["upm"], NT)
                elif i >= 3 and stream[i - 3][0] == "in":
                    t = ZQC * (stream[i - 3][1] + 1) - 1
                    sp.wait_ge(s_lo[t % NPAIR], t // NPAIR + 1)
                elif i >= 3:
                    sp.wait_ge(S["wdone"], stream[i - 3][1] + 1)
                dst = ring_slot[i % 3]
                if kind == "ada":
                    src = a["w_ada"].rearrange("o (k p) n -> p (o k) n", p=P)[:, :, m * CH:(m + 1) * CH]
                elif kind == "in":
                    c, n = (ZCHUNKS + GCHUNKS)[m]
                    src = a["w_in"].rearrange("o (k p) n -> p (o k) n", p=P)[:, :, c:c + n]
                    dst = dst[:, :, 0:n]
                elif kind in ("upr", "upa"):
                    w = a["w_up_r" if kind == "upr" else "w_up_a"]
                    src = w.rearrange("o (k p) n -> p (o k) n", p=P)
                    dst = at(ring, (i % 3) * SLOT, 4, D)
                else:
                    src = a["w_out"].rearrange("o (k p) n -> p (o k) n", p=P)[:, :, m * CH:(m + 1) * CH]
                sp.dma_start(dst, src).then_inc(s_wld[i % 3], 16)

            weights(("ada", 0))
            weights(("ada", 1))
            weights(("ada", 2))
            for j in range(NT):
                src = a["x_prompt"][0] if j == 0 else a["x_sample"][0, (j - 1) * P:j * P, :]
                sp.dma_start(xb[:, j, :], src).then_inc(s_xl[j], 16)
            sp.dma_start(nrm, a["norm1"].broadcast_to([P, D])).then_inc(S["n1"], 16)
            weights(("ada", 3))
            weights(("in", 0))
            weights(("in", 1))
            sp.wait_ge(S["modrow"], ADA1)
            sp.dma_start(mods_d[:, 0:ADA1 * CH], modrow[:, 0:ADA1 * CH]).then_inc(S["modd"], 16)
            sp.wait_ge(S["modd"], 16)
            for i in range(2):
                sp.dma_start(shb[:, i, :], mods_d[i:i + 1, 0:D].broadcast_to([P, D])).then_inc(S["modb1"], 16)
                sp.dma_start(scb[:, i, :], mods_d[i:i + 1, D:2 * D].broadcast_to([P, D])).then_inc(S["modb1"], 16)
            for m in range(2, NZ + 4):
                weights(("in", m))
            for m in range(ADA1, ADA):
                weights(("ada", m))
            sp.wait_ge(S["modrow"], ADA)
            sp.dma_start(mods_d[:, ADA1 * CH:], modrow[:, ADA1 * CH:]).then_inc(S["modd"], 16)
            for key in (("upr", 0), ("upa", 0), ("out", 0), ("out", 1)):
                weights(key)

            w1d, w2d = a["w_moe_in"][0], a["w_moe_out"][0]
            w1cols = [0, FF, CH, FF + CH]
            w1v = lambda e: w1d[e].rearrange("o (k p) n -> p (o k) n", p=P)
            w2v = lambda e: w2d[e].rearrange("o (k p) n -> p (o k) n", p=P)

            def expert_chunk(e, c):
                if c < W1C:
                    n = w1cols[c // 2]
                    src = w1v(e)[:, 4 * (c % 2):4 * (c % 2) + 4, n:n + CH]
                    dst = raw(c).rearrange("p (k n) -> p k n", k=4)
                else:
                    src = w2v(e)[:, 2 * (c - W1C):2 * (c - W1C) + 2, :]
                    dst = raw(c).rearrange("p (k n) -> p k n", k=2)
                sp.dma_start(dst, src).then_inc(s_es[c % NRAW], 16)

            sp.wait_ge(S["upm"], NT)
            for c in range(WC):
                if c == 2:
                    sp.wait_ge(S["wout"], 2 * NT)
                if c >= NRAW:
                    low_part_done(sp, 0, c - NRAW)
                expert_chunk(slice(0, 1), c)
            sp.wait_ge(S["routeq"], 8)
            nblk = sp.value_load(tab[0:1, 2 * P:2 * P + 1], min_val=NE, max_val=NBMAX)
            with sp.Fori(1, nblk) as it:
                e = sp.value_load(tab[0:1, bass.ds(it + P, 1)], min_val=0, max_val=NE - 1)
                for c in range(WC):
                    if c < NRAW:
                        low_part_done(sp, it - 1, c + WC - NRAW)
                    else:
                        low_part_done(sp, it, c - NRAW)
                    expert_chunk(bass.ds(e, 1), c)

            for j in range(NT):
                sp.wait_ge(S["fin"], j + 1)
                dst = o["y_prompt"][0] if j == 0 else o["y_sample"][0, (j - 1) * P:j * P, :]
                sp.dma_start(dst, x1[:, j, :]).then_inc(S["fout"], 16)
            sp.wait_ge(S["fout"], 16 * NT)
            sp.wait_ge(S["nkv"], 32)
            sp.wait_ge(S["sfout"], 32)

        @block.gpsimd
        def _(gp):
            gp.memset(at(ky, 0, D), 0.0).then_inc(S["chain2"], 1)
            gp.memset(half[:, :], -0.5).then_inc(S["chain2"], 1)
            gp.wait_ge(S["chain2"], 2)
            rs = ALU.pow
            for j in range(NT):
                gp.wait_ge(S["ssq"], j + 1)
                gp.tensor_tensor(stat[:, 8 + j:9 + j], stat[:, 4 + j:5 + j], half[:, 0:1], rs).then_inc(S["rstd"], 1)
            for j in range(NT):
                gp.wait_ge(S["anorm"], j + 1)
                gp.tensor_tensor(stat[:, 36:46], stat[:, 26:36], half[:, 0:10], rs).then_inc(S["arstd"], 1)
            for j in range(NT):
                gp.wait_ge(S["kkss"], j + 1)
                gp.tensor_tensor(stat[:, 16:24], stat[:, 8:16], half[:, 0:8], rs).then_inc(S["kkr"], 1)

            for u, (d, j) in enumerate(units):
                gp.wait_ge(S["kkd"], j + 1)
                gp.wait_ge(S["lexp"], 4 * u + 3)
                gp.tensor_tensor(RQ[:, 0, :], kkn[:, j, :], EQ, ALU.mult).then_inc(S["rqd"], 1)
                gp.tensor_tensor(RQ[:, 1, :], zbuf[:, j, ZR:ZR + DR], ER, ALU.mult).then_inc(S["rqd"], 1)

                def level(g, l):
                    if l == 0:
                        gp.wait_ge(S["am"], 8 * u + 4 * g + 4)
                    if l == 1 and u:
                        gp.wait_ge(s_p[g], 6 * u)
                    if l >= 2:
                        gp.wait_ge(s_p[g], 6 * u + l - 1)
                        gp.wait_ge(s_x[g], 6 * u + 1)
                    m = levelm[:, LEVELS * d + l:LEVELS * d + l + 1, :].broadcast_to([P, 4, P])
                    gp.tensor_tensor(ATL[g][l % 2], AM[:, 4 * g:4 * g + 4, 0, :], m, ALU.mult).then_inc(s_at[g], 1)

                for l in range(LEVELS):
                    for g in range(2):
                        level(g, l)
            for j in range(NT):
                gp.wait_ge(S["kkss"], NT + j + 1)
                gp.tensor_tensor(stat[:, 16:24], stat[:, 8:16], half[:, 0:8], rs).then_inc(S["kkr"], 1)
                if j < 2:
                    rows = slice((0, 2 * NE)[j], QMAX)
                    gp.wait_ge(S["b3d"], (1, 4)[j])
                    gp.wait_ge(S["kkr"], NT + j + 1)
                    gp.tensor_tensor(bias32[rows, :], bias32[rows, :], b3[rows, :], ALU.subtract).then_inc(S["b3d"], 1)
                    gp.wait_ge(S["b3d"], (2, 5)[j])
            for j in range(NT):
                gp.wait_ge(S["ssq"], NT + j + 1)
                gp.tensor_tensor(stat[:, 8 + j:9 + j], stat[:, 4 + j:5 + j], half[:, 0:1], rs).then_inc(S["rstd"], 1)

            def gather(count, prior):
                gp.wait_ge(S["idxc"], count)
                gp.wait_ge(S["h2out"], 16 * NT)
                if prior is not None:
                    gp.wait_ge(S["gpn"], prior)
                gp.tensor_tensor(half[:, 12:13], half[:, 13:14], half[:, 13:14], ALU.mult).then_inc(S["gpn"], 1)
                gp.indirect_dma_start(xg, None, h2_d, bass.IndirectOffsetOnAxis(ap=slots[:, 0:1], axis=0))\
                  .then_inc(S["xgd"], 16)

            for c in range(NPAIR - 1):
                low_part(gp, 0, c)
            gather(1, None)
            low_part(gp, 0, NPAIR - 1)
            gp.wait_ge(S["routeq"], 8)
            last_it = gp.value_load(tab[0:1, 2 * P + 1:2 * P + 2], min_val=NE - 1, max_val=NBMAX - 1)

            def block_of(it, last):
                low_part(gp, it, 5)
                if not last:
                    gp.wait_ge(S["xtm"], 2 * it + 2)
                    gather(it + 2, it + 1)
                low_part(gp, it, 9)
                if not last:
                    low_part(gp, it, WC + 1)

            with gp.Fori(0, last_it) as it:
                block_of(it, False)
            block_of(last_it, True)
            gp.wait_ge(S["yo"], 16 * last_it + 32)
            gp.wait_ge(S["gpn"], last_it + 1)
            gp.tensor_tensor(half[:, 12:13], half[:, 13:14], half[:, 13:14], ALU.mult)
            for n in range(NT * TOPK):
                gp.indirect_dma_start(ygat[n], None, rows_d,
                                      bass.IndirectOffsetOnAxis(ap=dest[:, n:n + 1], axis=0))\
                  .then_inc(s_yg[n // TOPK], 16)
            for j in range(NT):
                gp.wait_ge(S["ssq"], 2 * NT + j + 1)
                gp.tensor_tensor(stat[:, 8 + j:9 + j], stat[:, 4 + j:5 + j], half[:, 0:1], rs).then_inc(S["rstd"], 1)

        @block.tensor
        def _(pe):
            def mm(out, l, r, start=True, stop=True):
                return pe.matmul(out, l, r, start=start, stop=stop)

            def mm_part(out, l, r, start=True, stop=True):
                return pe.matmul(out, l, r, start=start, stop=stop, skip_group_check=True)

            def tr(out, src, n=P):
                return pe.transpose(out, src, ident[0:n, 0:n])

            pe.wait_ge(S["cond"], 48)
            tr(B[7][:, 0:16], condc[:, :], 16).then_inc(S["condq"], 1)
            pe.wait_ge(S["condq"], 4)

            def modulation(m, ks=range(KC)):
                for k in ks:
                    if k == 0:
                        landed(pe, ("ada", m))
                        if m >= 2:
                            pe.wait_ge(S["modrow"], m - 1)
                    ins = mm(ada_bank(m)[0:2, :], condT[:, k, :], ring_slot[turn["ada", m] % 3][:, k, :],
                             k == 0, k == KC - 1)
                    if k == KC - 1:
                        ins.then_inc(S["wdone"], 1)

            for m in range(ADA1):
                modulation(m)
            for j in range(NT):
                pe.wait_ge(S["htok"], j + 1)
                if j == 2:
                    pe.wait_ge(S["hTv"], 2)
                for k in range(KC):
                    bank = B[2 * (j % 2) + k // 4]
                    last = tr(bank[:, (k % 4) * P:(k % 4 + 1) * P], xb[:, j, k * P:(k + 1) * P])
                    if k % 4 == 3:
                        last.then_inc(S["htr"], 1)
            pe.wait_ge(S["hTv"], 2 * NT)
            for t in range(ZQ_ALL):
                m, q = t // ZQC, t % ZQC
                n = (ZCHUNKS + GCHUNKS)[m][1]
                pe.wait_ge(s_lo[t % NPAIR], t // NPAIR + 1)
                w = [zpart(t, i, n) for i in range(2)]
                for j in range(NT):
                    i = NT * m + j
                    if q == 0 and i >= 6:
                        z_evacuated(pe, i - 6)
                    for k in range(KQ):
                        for xi, wi in ((0, 0), (0, 1), (1, 0)):
                            first, last = q == k == xi == wi == 0, q == ZQC - 1 and k == KQ - 1 and xi == 1
                            ins = mm(B[i % 6][:, 0:n], hTp[xi][:, KQ * q + k, j * P:(j + 1) * P], w[wi][:, k, :],
                                     first, last)
                    if q == ZQC - 1 and j < NT - 1:
                        ins.then_inc(S["zmm"], 1)
                ins.then_inc(S["mult"], 1)
            for m in range(ADA1, ADA2):
                modulation(m)
            for i in range(len(zunits) - 6, len(zunits)):
                z_evacuated(pe, i)

            for j in range(NT + 1):
                if j < NT:
                    pe.wait_ge(S["aqk"], j + 1)
                    if j:
                        pe.wait_ge(S["qTa"], j)
                    for c in range(4):
                        last = tr(B[0][:, c * P:(c + 1) * P], qk[:, j, 2 * c:2 * c + 2, :])
                    last.then_inc(S["qtr"], 1)
                pe.wait_ge(S["kdupd"], j + 1)
                if j:
                    pe.wait_ge(S["kTv"], j)
                for g in range(NKV):
                    last = tr(B[1][:, g * P:(g + 1) * P], kdup[:, 2 * g:2 * g + 2, :])
                last.then_inc(S["ktr"], 1)
            pe.wait_ge(S["qTa"], NT)
            pe.wait_ge(S["kTv"], NT + 1)
            pe.wait_ge(S["modrow"], ADA2)

            def modulation_step(i):
                if i < (ADA - ADA2) * KC:
                    modulation(ADA2 + i // KC, [i % KC])

            def scores(n):
                j, h = aunits[n]
                base, c, g = HD * (h % 2), h // 2, h // (NHQ // NKV)
                keys = KT[base:base + HD, g, 0:P] if j == 0 else KT[base:base + HD, g, P:4 * P]
                if n >= 2:
                    pe.wait_ge(S["prob"], n - 1)
                mm(B[2 + n % 2][:, 0:P if j == 0 else 3 * P], QT[base:base + HD, c, j * P:(j + 1) * P], keys)\
                    .then_inc(S["smm"], 1)

            def turn_probs(n):
                nb = 1 if aunits[n][0] == 0 else 3
                pe.wait_ge(S["prob"], n + 1)
                if n >= 2:
                    pe.wait_ge(S["ptc"], n - 1)
                for b in range(nb):
                    last = tr(B[4 + n % 2][:, b * P:(b + 1) * P], prob[:, n % 2, b * P:(b + 1) * P])
                last.then_inc(S["ptr"], 1)

            def values(n):
                j, h = aunits[n]
                g = h // (NHQ // NKV)
                pe.wait_ge(S["ptc"], n + 1)
                if n >= 2:
                    pe.wait_ge(S["ya"], n - 1)
                if n == 0:
                    pe.wait_ge(S["cachekv"], 32)
                tiles = [0] if j == 0 else [1, 2, None]
                for b, t in enumerate(tiles):
                    v = ckv[:, 1, g * HD:(g + 1) * HD] if t is None else zbuf[:, t, ZVA + g * HD:ZVA + (g + 1) * HD]
                    last = mm(B[6 + n % 2][:, 0:HD], probT[:, n % 2, b * P:(b + 1) * P], v, b == 0, b == len(tiles) - 1)
                last.then_inc(S["pv"], 1)

            for n in range(len(aunits) + 2):
                modulation_step(2 * n)
                if n < len(aunits):
                    scores(n)
                if 1 <= n <= len(aunits):
                    turn_probs(n - 1)
                modulation_step(2 * n + 1)
                if n >= 2:
                    values(n - 2)
            pe.wait_ge(S["ya"], len(aunits))
            pe.wait_ge(S["modrow"], ADA)

            pe.wait_ge(S["tg"], 2)
            pe.wait_ge(S["sgd"], 1)
            for i, c in enumerate((ZWD, ZAD, ZGD)):
                for j in range(NT):
                    last = tr(B[i][:, j * P:(j + 1) * P], zbuf[:, j, c:c + P])
                last.then_inc(S["ttr"], 1)
            for d in range(2):
                pe.wait_ge(S["stld"], 32)
                if d:
                    pe.wait_ge(S["stev"], 1)
                for c in range(4):
                    last = tr(B[3][:, c * HD:(c + 1) * HD], stin[d][:, c * P:(c + 1) * P], HD)
                last.then_inc(S["sttr"], 1)
            pe.wait_ge(S["tcA"], 2)
            pe.wait_ge(S["tcV"], 1)
            pe.wait_ge(S["stev"], 2)
            pe.wait_ge(S["cons2"], 16 * NCONS2)

            for u, (d, j) in enumerate(units):
                lat = j > 0
                lo = 64 * d
                for i, (src, w) in enumerate(((twT, w2s), (adT, a2s))):
                    mm(B[i], src[lo:lo + 64, j * P:(j + 1) * P], w[lo:lo + 64, :]).then_inc(S["lora"], 1)
                pe.wait_ge(S["lw"], u + 1)
                pe.wait_ge(S["lt1"], 2 * u + 2)
                mm(B[0], cum[:, 2 * d, :], LW).then_inc(S["lcum"], 1)
                mm(B[1], cum[:, 2 * d + 1, :], LW).then_inc(S["lcum"], 1)
                for c in range(4):
                    last = mm(B[2][:, 2 * c:2 * c + 2], LW[:, c * P:(c + 1) * P], colm[:, 2 * d:2 * d + 2])
                last.then_inc(S["lcum"], 1)
                if u:
                    pe.wait_ge(S["yrd"], 2 * u)
                    pe.wait_ge(S["st2"], st_index[u])
                for i in range(4):
                    if i < 2:
                        pe.wait_ge(S["rqd"], 2 * u + i + 1)
                        src = RQ[:, i, :]
                    else:
                        pe.wait_ge(S["bkd"], 2 * u + i - 1)
                        src = (BT_, KT_)[i - 2]
                    for c in range(4):
                        last = tr(B[3 + i][:, c * P:(c + 1) * P], src[:, c * P:(c + 1) * P])
                    last.then_inc(S["ttr4"], 1)
                pe.wait_ge(S["rqT"], 2 * u + 2)
                pe.wait_ge(S["bkT"], 2 * u + 2)
                pe.wait_ge(S["lexp"], 4 * u + 4)
                for h in range(HR):
                    base, c = HD * (h % 2), h // 2
                    qr = QRT[base:base + HD, c, :, :]
                    mm(B[gbank[h]][:, 0:2 * P], BTT[base:base + HD, c, :], qr)
                    mm(B[gbank[h]][:, 2 * P:4 * P], KTT[base:base + HD, c, :], qr).then_inc(S["gram"], 1)
                pe.wait_ge(S["am"], 8 * u + 8)

                def heads(g):
                    return [(x, 4 * g + x) for x in range(4)]

                for l in range(LEVELS - 1):
                    for g in range(2):
                        bp = B[2 + 3 * g]
                        pe.wait_ge(s_at[g], 7 * u + l + 1)
                        if l:
                            pe.wait_ge(s_x[g], 6 * u + l)
                        for x, _ in heads(g):
                            last = mm(bp[:, x * P:(x + 1) * P], ATL[g][l % 2][:, x, :],
                                      XM[g][:, x, :] if l else ident[:, :])
                        last.then_inc(s_p[g], 1)
                    if l == 0:
                        continue
                    for g in range(2):
                        bd, bdt = B[3 + 3 * g], B[4 + 3 * g]
                        pe.wait_ge(s_pc[g], 5 * u + l)
                        for x, _ in heads(g):
                            if l < LEVELS - 2:
                                mm(bd[:, x * P:(x + 1) * P], XT[g][:, x, :], PM[g][:, x, :])
                            last = mm(bdt[:, x * P:(x + 1) * P], PM[g][:, x, :], XT[g][:, x, :])
                        last.then_inc(s_d[g], 1)
                vh = lambda h: zbuf[:, j, ZV + h * HD:ZV + (h + 1) * HD]
                if lat:
                    pe.wait_ge(S["s0p"], lat_index[u] + 1)
                for g in range(2):
                    for x, h in heads(g):
                        if lat and x % 2 == 0:
                            mm_part(B[2 + 3 * g][:, x * HD:(x + 2) * HD], QRT[:, h // 2, 0, :], S0P[:, h // 2, :, :],
                                    True, False)
                        last = mm_part(B[2 + 3 * g][:, x * HD:(x + 1) * HD], AM[:, h, 2, :], vh(h), not lat, True)
                    last.then_inc(s_u[g], 1)
                for g in range(2):
                    pe.wait_ge(s_uc[g], 4 * u + 1)
                    pe.wait_ge(s_x[g], 6 * u + 6)
                    for x, h in heads(g):
                        last = mm(B[3 + 3 * g][:, x * HD:(x + 1) * HD], XT[g][:, x, :], GM[g][:, x, :])
                    last.then_inc(s_u[g], 1)
                for g in range(2):
                    pe.wait_ge(s_uc[g], 4 * u + 2)
                    pe.wait_ge(s_at[g], 7 * u + 7)
                    for x, h in heads(g):
                        last = mm(B[4 + 3 * g][:, x * HD:(x + 1) * HD], ATL[g][0][:, x, :], U1[g][:, x, :])
                    last.then_inc(s_u[g], 1)
                for g in range(2):
                    pe.wait_ge(s_uc[g], 4 * u + 3)
                    for x, h in heads(g):
                        last = mm(B[2 + 3 * g][:, x * HD:(x + 1) * HD], XT[g][:, x, :], U2[g][:, x, :])
                    last.then_inc(s_u[g], 1)
                for g in range(2):
                    pe.wait_ge(s_uc[g], 4 * u + 4)
                    for x, h in heads(g):
                        out = B[3 + 3 * g][:, x * HD:(x + 1) * HD]
                        if lat and x % 2 == 0:
                            mm_part(B[3 + 3 * g][:, x * HD:(x + 2) * HD], QRT[:, h // 2, 1, :], S0P[:, h // 2, :, :],
                                    True, False)
                        mm_part(out, AM[:, h, 1, :], UU[g][:, x, :], not lat, False)
                        last = mm_part(out, AM[:, h, 3, :], vh(h), False, True)
                    last.then_inc(S["yout"], 1)
                    if u not in LAST:
                        for x, h in heads(g):
                            base = HD * (h % 2)
                            out = B[4 + 3 * g][base:base + HD, (x // 2) * HD:(x // 2 + 1) * HD]
                            mm(out, BT_[:, h * HD:(h + 1) * HD], UU[g][:, x, :], True, False)
                            last = mm(out, KT_[:, h * HD:(h + 1) * HD], vh(h), False, True)
                        last.then_inc(S["twod"], 1)
                if not lat:
                    pe.wait_ge(S["st2"], st_index[u] + 2)
                    for c in range(4):
                        last = tr(B[0][0:HD, c * P:(c + 1) * P], sfin[:, c, :])
                    last.then_inc(S["sftr"], 1)
                    pe.wait_ge(S["sfcp"], CTX.index(u) + 1)
            pe.wait_ge(S["yrd"], 2 * NU)

            for j in range(NT):
                if j:
                    pe.wait_ge(S["yfin"], j)
                mm(B[6], sgT[:, j * P:(j + 1) * P], g2s).then_inc(S["gps"], 1)
                pe.wait_ge(S["yfin"], j + 1)
                if j:
                    pe.wait_ge(S["yTc"], 2 * j)
                    pe.wait_ge(S["mTc"], 2 * j)
                for c in range(4):
                    last = tr(B[7][:, c * P:(c + 1) * P], yc[:, c * P:(c + 1) * P])
                last.then_inc(S["ytr"], 1)
                for c in range(4):
                    last = tr(B[5][:, c * P:(c + 1) * P], zbuf[:, j, ZQ + c * P:ZQ + (c + 1) * P])
                last.then_inc(S["ytr"], 1)
                pe.wait_ge(S["yTc"], 2 * j + 2)
                if j:
                    pe.wait_ge(S["mrg"], j)
                for i, (key, src) in enumerate((("upr", yrT), ("upa", yaT))):
                    if j == 0:
                        landed(pe, (key, 0))
                    w = at(ring, (turn[key, 0] % 3) * SLOT, 4, D)
                    for n in range(2):
                        for k in range(4):
                            last = mm(B[2 * i + n], src[:, k, j * P:(j + 1) * P], w[:, k, n * CH:(n + 1) * CH],
                                      k == 0, k == 3)
                last.then_inc(S["upm"], 1)
                pe.wait_ge(S["mrg"], j + 1)
                for k in range(KC):
                    last = tr(B[4 + k // 4][:, (k % 4) * P:(k % 4 + 1) * P], mg[:, k * P:(k + 1) * P])
                    if k % 4 == 3:
                        last.then_inc(S["mtr"], 1)
            pe.wait_ge(S["mTc"], 2 * NT)
            for j in range(NT):
                if j == 2:
                    pe.wait_ge(S["x1s"], 1)
                for n in range(2):
                    if j == 0:
                        landed(pe, ("out", n))
                    w = ring_slot[turn["out", n] % 3]
                    for k in range(KC):
                        last = mm(B[2 * (j % 2) + n], mT[:, k, j * P:(j + 1) * P], w[:, k, :], k == 0, k == KC - 1)
                    last.then_inc(S["wout"], 1)
            for j in range(NT):
                pe.wait_ge(S["h2s"], j + 1)
                if j:
                    pe.wait_ge(S["h2Tc"], 2 * j)
                for k in range(KC):
                    last = tr(B[4 + k // 4][:, (k % 4) * P:(k % 4 + 1) * P], h2[:, k * P:(k + 1) * P])
                    if k % 4 == 3:
                        last.then_inc(S["h2tr"], 1)
                pe.wait_ge(S["h2Tc"], 2 * j + 2)
                for k in range(KC):
                    last = mm(B[6][:, j * NE:(j + 1) * NE], h2T[:, k, :], wrout[:, k, :], k == 0, k == KC - 1)
                last.then_inc(S["lg"], 1)

            pe.wait_ge(S["routeq"], 1)
            pe.wait_ge(S["cons3"], 16 * (NCONS3 + NCONS4))
            for j in range(NT):
                for i in range(j + 1):
                    last = mm(B[7][:, j * NE:(j + 1) * NE], crank[:, 0:P] if i == j else crank[:, P:2 * P],
                              selm[:, i, :], i == 0, i == j)
            last.then_inc(S["routeq"], 1)
            for q in range(NB):
                for j in range(NT):
                    last = mm(B[5][q * NE:(q + 1) * NE, 0:1], selm[:, j, :], crank[:, P:P + 1], j == 0, j == NT - 1)
            last.then_inc(S["routeq"], 1)
            pe.wait_ge(S["routeq"], 4)
            mm(B[4][0:QMAX, 0:1], crank[0:QMAX, 0:QMAX], acol)
            mm(B[4][:, P:P + QMAX], aspread, crank[0:QMAX, 0:QMAX]).then_inc(S["routeq"], 1)
            pe.wait_ge(S["routeq"], 6)
            mm(B[3][0:1, 0:P], cq[0:QMAX, 0:1], lsto)
            mm(B[3][0:1, P:2 * P], cq[0:QMAX, 1:2], lsto)
            mm(B[3][0:1, 2 * P:2 * P + 1], acol, cq[0:QMAX, 3:4]).then_inc(S["routeq"], 1)

            hb, yb, t0, t1 = B[0:4], B[4:6], B[6], B[7]

            def list_tokens(count):
                pe.wait_ge(S["cmpd"], count)
                for j in range(NT):
                    last = mm(t1[:, 0:1], cmp[:, j, :], ctok[:, j:j + 1], j == 0, j == NT - 1)
                last.then_inc(S["idxm"], 1)

            def turn_rows(half_):
                for k in range(4 * half_, 4 * half_ + 4):
                    last = tr(t1[:, (k % 4) * P:(k % 4 + 1) * P], xg[:, k * P:(k + 1) * P])
                last.then_inc(S["xtm"], 1)

            def chunk(it, c, out, x, k0, n0, n, first=False, last=False):
                w = [part(c, i).rearrange("p (k n) -> p k n", n=n) for i in range(2)]
                for k in range(CW // n):
                    for xi, wi in ((0, 0), (0, 1), (1, 0)):
                        ins = mm(out, x[xi][:, k0 + k, :], w[wi][:, k, n0:n0 + CH], False,
                                 last and k == CW // n - 1 and xi == 1)
                return ins

            def bias(out, e, n):
                mm(out, selc[0:QMAX, bass.ds(e, 1), :].rearrange("p a t -> p (a t)"), b3[0:QMAX, n:n + CH], True, False)

            def turn_act(it, h):
                pe.wait_ge(S["actd"], 2 * it + (h + 3))
                for k in range(4):
                    last = tr(t0[:, k * P:(k + 1) * P], act[:, (4 * h + k) * P:(4 * h + k + 1) * P])
                last.then_inc(S["atm"], 1)

            list_tokens(1)
            pe.wait_ge(S["xgd"], 16)
            turn_rows(0)
            pe.wait_ge(S["xtl"], 1)
            turn_rows(1)
            pe.wait_ge(S["b3d"], 6)
            pe.wait_ge(S["selld"], 16)
            last_it = pe.value_load(tab[0:1, 2 * P + 1:2 * P + 2], min_val=NE - 1, max_val=NBMAX - 1)

            def block_of(it, last):
                e = pe.value_load(tab[0:1, bass.ds(it + P, 1)], min_val=0, max_val=NE - 1)
                pe.wait_ge(S["xtl"], 2 * it + 2)
                for c in range(W1C):
                    if c % 4 == 0:
                        pe.wait_ge(S["actd"], 2 * it + (c // 4 + 1))
                    if c % 2 == 0:
                        bias(hb[c // 2], e, (c // 4) * CH + (c // 2 % 2) * FF)
                    low_part_done(pe, it, c)
                    chunk(it, c, hb[c // 2], xTp, 4 * (c % 2), 0, CH, last=c % 2 == 1).then_inc(S["mult"], 1)
                    if c == 3 and not last:
                        list_tokens(it + 2)
                    if c == 5:
                        turn_act(it, 0)
                if not last:
                    pe.wait_ge(S["xgd"], 16 * it + 32)
                    turn_rows(0)
                pe.wait_ge(S["atl"], 2 * it + 1)
                pe.wait_ge(S["yc"], 2 * it + 2)
                for n in range(2):
                    bias(yb[n], e, 2 * FF + n * CH)
                for c in range(W1C, WC):
                    if c == W1C + 2:
                        pe.wait_ge(S["atl"], 2 * it + 2)
                    low_part_done(pe, it, c)
                    for n in range(2):
                        ins = chunk(it, c, yb[n], actTp, 2 * (c - W1C), n * CH, D, last=c == WC - 1)
                        if n == 0 and c == WC - 1:
                            ins.then_inc(S["ymm"], 1)
                    ins.then_inc(S["mult"], 1)
                    if c == W1C:
                        turn_act(it, 1)
                        if not last:
                            pe.wait_ge(S["xtl"], 2 * it + 3)
                            turn_rows(1)

            with pe.Fori(0, last_it) as it:
                block_of(it, False)
            block_of(last_it, True)

        @block.scalar
        def _(sc):
            cp = lambda out, src, scale=1.0: sc.activation(out, src, ACT.Copy, scale=scale)
            sc.sem_inc(S["yc"], 2)
            sc.sem_inc(S["yo"], 16)
            sc.wait_ge(S["condq"], 2)
            sc.activation(condf[:, 1, :], condf[:, 0, :], ACT.Tanh, scale=0.5).then_inc(S["condq"], 1)
            for j in range(NT):
                for i in range(2):
                    sc.wait_ge(S["htr"], 2 * j + i + 1)
                    cp(hTp[0][:, 4 * i:4 * i + 4, j * P:(j + 1) * P], B[2 * (j % 2) + i].rearrange("p (k t) -> p k t", k=4))\
                        .then_inc(S["hTa"], 1)
            sc.wait_ge(S["htok"], NT)
            for i, name in enumerate(("q_norm", "k_norm")):
                sc.dma_start(gqk[:, i, :], a[name].broadcast_to([P, HD])).then_inc(S["cons3"], 16)
            for i, name in enumerate(("cache_k", "cache_v")):
                sc.dma_start(ckv[:, i, :], a[name][0, 0].rearrange("t g d -> t (g d)")).then_inc(S["cachekv"], 16)
            for dst, src in cons2:
                sc.dma_start(dst, src).then_inc(S["cons2"], 16)
            sc.wait_ge(S["chain2"], 1)
            for i in range(NEXTRA):
                sc.dma_start(rows_d[(NE + i) * P:(NE + i + 1) * P, :], at(ky, 0, D)).then_inc(S["zfill"], 16)
            sc.wait_ge(S["htr"], 2 * NT)
            for i in z_order(lambda t: z_high(sc, t)):
                m, j = zunits[i]
                if m < NZ and i % 2:
                    continue
                c, n = (ZCHUNKS + GCHUNKS)[m]
                z_multiplied(sc, i)
                if m < NZ:
                    cp(zbuf[:, j, c:c + n], B[i % 6][:, 0:n]).then_inc(S["zA"], 1)
                    continue
                r = i - NZ * NT
                if r >= 4:
                    sc.wait_ge(s_gst[r % 4], 16 * (r // 4))
                sc.activation(gst[:, r % 4, :], B[i % 6], ACT.Tanh, scale=0.5).then_inc(S["zA"], 1)
                z_evacuated(sc, i)
                sc.dma_start(gates_d[j, :, (m - NZ) * CH:(m - NZ + 1) * CH], gst[:, r % 4, :]).then_inc(s_gst[r % 4], 16)
            z_evacuated(sc, NZ * NT - 1)
            sc.activation(zbuf[:, :, ZWD:ZWD + P], zbuf[:, :, ZWD:ZWD + P], ACT.Tanh).then_inc(S["tg"], 1)
            sc.activation(zbuf[:, :, ZGD:ZGD + P], zbuf[:, :, ZGD:ZGD + P], ACT.Tanh, scale=0.5).then_inc(S["tg"], 1)
            for g in range(4):
                sc.wait_ge(s_gst[g], 48)
            for j in range(NT):
                sc.wait_ge(S["qtr"], j + 1)
                cp(QT[:, :, j * P:(j + 1) * P], B[0].rearrange("p (k t) -> p k t", k=4)).then_inc(S["qTa"], 1)
            sc.dma_start(o["new_cache_k"][0, 0].rearrange("t g d -> t (g d)"),
                         qk[:, 0, NHQ:NQK, :].rearrange("p g d -> p (g d)")).then_inc(S["nkv"], 16)
            sc.dma_start(o["new_cache_v"][0, 0].rearrange("t g d -> t (g d)"),
                         zbuf[:, 0, ZVA:ZVA + P]).then_inc(S["nkv"], 16)
            for i, name in enumerate(("state_rwkv_fwd", "state_rwkv_bwd")):
                sc.dma_start(stin[i].rearrange("v (h k) -> v h k", h=HR),
                             a[name][0, 0].rearrange("h v k -> v h k")).then_inc(S["stld"], 16)

            def softmax(n):
                nk = P if aunits[n][0] == 0 else 3 * P
                sc.wait_ge(S["nmax"], n + 1)
                if n >= 2:
                    sc.wait_ge(S["ptr"], n - 1)
                    sc.wait_ge(S["rinv"], n - 1)
                sc.activation(prob[:, n % 2, 0:nk], B[2 + n % 2][:, 0:nk], ACT.Exp, scale=SCALE,
                              bias=stat[:, 50 + n % 2:51 + n % 2],
                              accum_out=stat[:, 52 + n % 2:53 + n % 2]).then_inc(S["prob"], 1)

            def weigh(n):
                j, h = aunits[n]
                sc.wait_ge(S["pv"], n + 1)
                sc.wait_ge(S["rinv"], n + 1)
                cp(zbuf[:, j, ZQ + h * HD:ZQ + (h + 1) * HD], B[6 + n % 2][:, 0:HD],
                   stat[:, 54 + n % 2:55 + n % 2]).then_inc(S["ya"], 1)

            for n in range(len(aunits) + 2):
                if n < len(aunits):
                    softmax(n)
                if n >= 2:
                    weigh(n - 2)

            for i, dst in ((0, twT), (2, sgT)):
                sc.wait_ge(S["ttr"], i + 1)
                cp(dst, B[i][:, 0:NT * P]).then_inc(S["tcA"], 1)
            for u, (d, j) in enumerate(units):
                for i, t in enumerate((T1, T2)):
                    sc.wait_ge(S["lt1"], 2 * u + i + 1)
                    sc.activation(t, t, ACT.Tanh, scale=0.5).then_inc(S["ltanh"], 1)
                sc.wait_ge(S["lcum"], 3 * u + 1)
                sc.activation(ER, B[0], ACT.Exp).then_inc(S["lexp"], 1)
                sc.activation(EN, B[0], ACT.Exp, scale=-1.0).then_inc(S["lexp"], 1)
                sc.wait_ge(S["lcum"], 3 * u + 2)
                sc.activation(EQ, B[1], ACT.Exp).then_inc(S["lexp"], 1)
                sc.wait_ge(S["lcum"], 3 * u + 3)
                sc.activation(ecol.rearrange("p a b -> p (a b)"), B[2][:, 0:8], ACT.Exp).then_inc(S["lexp"], 1)
                for i in range(2):
                    sc.wait_ge(S["ttr4"], 4 * u + i + 1)
                    cp(QRT[:, :, i, :], B[3 + i].rearrange("p (k t) -> p k t", k=4)).then_inc(S["rqT"], 1)
                for l in range(1, LEVELS - 1):
                    for g in range(2):
                        sc.wait_ge(s_p[g], 6 * u + l + 1)
                        cp(PM[g].rearrange("p a b -> p (a b)"), B[2 + 3 * g]).then_inc(s_pc[g], 1)
                for i, (dst, b) in enumerate(((GM, 2), (U1, 3), (U2, 4))):
                    for g in range(2):
                        sc.wait_ge(s_u[g], 4 * u + i + 1)
                        cp(dst[g].rearrange("p a b -> p (a b)"), B[b + 3 * g][:, 0:4 * HD]).then_inc(s_uc[g], 1)
                if u in CTX:
                    i = CTX.index(u)
                    sc.wait_ge(S["sftr"], i + 1)
                    if i:
                        sc.wait_ge(S["sfout"], 16)
                    cp(stout[:, :], B[0][0:HD, :]).then_inc(S["sfcp"], 1)
                    sc.wait_ge(S["sfcp"], i + 1)
                    dst = o["new_state_fwd" if d == 0 else "new_state_bwd"]
                    sc.dma_start(dst[0, 0].rearrange("h v k -> v h k"),
                                 stout[:, :].rearrange("v (h k) -> v h k", h=HR)).then_inc(S["sfout"], 16)
            sc.wait_ge(S["yrd"], 2 * NU)
            for dst, src in ((lnw, "rw_ln_w"), (lnb, "rw_ln_b")):
                sc.dma_start(dst, a[src].broadcast_to([P, DR])).then_inc(S["lnld"], 16)
            sc.dma_start(selc[0:QMAX, :, :].rearrange("p e t -> p (e t)").bitcast(U16), a["c_sel"]).then_inc(S["selld"], 16)
            sc.dma_start(gld, gates_d[0]).then_inc(S["gld"], 16)
            sc.dma_start(n2, a["norm2"].broadcast_to([P, D])).then_inc(S["n1"], 16)

            def cond_rows(i):
                sc.dma_start(g1b, mods_d[i:i + 1, 2 * D:3 * D].broadcast_to([P, D])).then_inc(S["g1l"], 16)

            def x_rows(j):
                src = a["x_prompt"][0] if j == 0 else a["x_sample"][0, (j - 1) * P:j * P, :]
                sc.dma_start(xr2, src).then_inc(s_xl[j], 16)

            def norm2_rows(i):
                sc.dma_start(sh2, mods_d[i:i + 1, 3 * D:4 * D].broadcast_to([P, D])).then_inc(S["n2l"], 16)
                sc.dma_start(sc2, mods_d[i:i + 1, 4 * D:5 * D].broadcast_to([P, D])).then_inc(S["n2l"], 16)

            for q in range(NB):
                sc.dma_start(bias32[q * NE:(q + 1) * NE, 0:2 * FF], a["b_moe_in"][0]).then_inc(S["b32"], 16)
                sc.dma_start(bias32[q * NE:(q + 1) * NE, 2 * FF:3 * FF], a["b_moe_out"][0]).then_inc(S["b32"], 16)
            sc.wait_ge(S["modd"], 32)
            cond_rows(0)
            x_rows(0)
            sc.wait_ge(S["b32"], 16 * 2 * NB)
            cp(b3[0:QMAX, :], bias32[0:QMAX, :]).then_inc(S["b3d"], 1)
            for j in range(NT):
                if j == 1:
                    sc.wait_ge(S["b3d"], 2)
                    cp(b3[NE:2 * NE, :], bias32[NE:2 * NE, :]).then_inc(S["b3d"], 1)
                    cp(b3[2 * NE:QMAX, :], bias32[2 * NE:QMAX, :]).then_inc(S["b3d"], 1)
                if j == 2:
                    sc.wait_ge(S["b3d"], 5)
                    cp(b3[2 * NE:QMAX, :], bias32[2 * NE:QMAX, :]).then_inc(S["b3d"], 1)
                    sc.wait_ge(S["b3d"], 6)
                    norm2_rows(0)
                for i, dst in enumerate((yrT, yaT)):
                    sc.wait_ge(S["ytr"], 2 * j + i + 1)
                    cp(dst[:, :, j * P:(j + 1) * P], B[(7, 5)[i]].rearrange("p (k t) -> p k t", k=4)).then_inc(S["yTc"], 1)
                for i in range(2):
                    sc.wait_ge(S["mtr"], 2 * j + i + 1)
                    cp(mT[:, 4 * i:4 * i + 4, j * P:(j + 1) * P], B[4 + i].rearrange("p (k t) -> p k t", k=4), 0.5)\
                        .then_inc(S["mTc"], 1)
                if j + 1 < NT:
                    sc.wait_ge(S["mrg"], j + 1)
                    sc.dma_start(gld, gates_d[j + 1]).then_inc(S["gld"], 16)
            sc.wait_ge(S["yfin"], NT)
            for dst, src in ((crank, a["c_rank"]), (iota, a["c_iota"]), (ctok, a["c_tok"]), (cq, a["c_q"]),
                             (brow, a["b_router"].broadcast_to([P, NE]))):
                sc.dma_start(dst, src).then_inc(S["cons3"], 16)
            for j in range(1, NT):
                sc.wait_ge(S["x1s"], j)
                x_rows(j)
                if j == 1:
                    cond_rows(1)
            for j in range(NT):
                sc.wait_ge(S["h2s"], j + 1)
                sc.dma_start(h2_d[j * P:(j + 1) * P, :], h2).then_inc(S["h2out"], 16)
                if j == 0:
                    norm2_rows(1)
                for i in range(2):
                    sc.wait_ge(S["h2tr"], 2 * j + i + 1)
                    if j:
                        sc.wait_ge(S["lg"], j)
                    cp(h2T[:, 4 * i:4 * i + 4, :], B[4 + i].rearrange("p (k t) -> p k t", k=4)).then_inc(S["h2Tc"], 1)
            sc.wait_ge(S["exa"], 1)
            sc.activation(exd, exd, ACT.Exp).then_inc(S["exb"], 1)
            for c in range(NPAIR):
                high_part(sc, 0, c, free=False)

            def listed(count):
                sc.wait_ge(S["idxm"], count)
                cp(slots[:, :], B[7][:, 0:1]).then_inc(S["idxc"], 1)

            def rows_turned(half_, count):
                sc.wait_ge(S["xtm"], count)
                cp(xTp[0][:, 4 * half_:4 * half_ + 4, :], B[7].rearrange("p (k t) -> p k t", k=4)).then_inc(S["xtc"], 1)

            listed(1)
            rows_turned(0, 1)
            rows_turned(1, 2)
            sc.wait_ge(S["routeq"], 8)
            last_it = sc.value_load(tab[0:1, 2 * P + 1:2 * P + 2], min_val=NE - 1, max_val=NBMAX - 1)
            rows_q = rows_d.rearrange("(q t) n -> q t n", t=P)

            def block_of(it, last):

                def sigmoid(h):
                    sc.wait_ge(S["gld2"], 2 * it + (h + 1))
                    sc.activation(th, gl, ACT.Tanh, scale=ALPHA / 2).then_inc(S["thd"], 1)

                def act_turned(h):
                    sc.wait_ge(S["atm"], 2 * it + (h + 1))
                    cp(actTp[0][:, 4 * h:4 * h + 4, :], B[6].rearrange("p (k t) -> p k t", k=4), 0.5).then_inc(S["atc"], 1)

                for c in range(NPAIR, WC if last else WC + NPAIR):
                    high_part(sc, it, c)
                    if c == 5:
                        sigmoid(0)
                        if not last:
                            sc.wait_ge(S["xgd"], 16 * it + 16)
                            listed(it + 2)
                    if c == 9:
                        act_turned(0)
                        sigmoid(1)
                    if c == 10 and not last:
                        rows_turned(0, 2 * it + 3)
                    if c == 11:
                        act_turned(1)
                        if not last:
                            rows_turned(1, 2 * it + 4)
                if last:
                    sc.wait_ge(S["cmpd"], last_it + 1)
                    for dst, src in ((nfb, a["norm_f"].rearrange("(o n) -> o n", o=1)),
                                     (g2b[0], mods_d[0:1, 5 * D:6 * D]), (g2b[1], mods_d[1:2, 5 * D:6 * D])):
                        sc.dma_start(dst, src.broadcast_to([P, D])).then_inc(S["fld"], 16)
                sc.wait_ge(S["mult"], WC * it + (WC + ZQ_ALL))
                sc.wait_ge(S["yo"], 16 * it + 16)
                cp(ysb[:, CH:D], B[5]).then_inc(S["yc"], 1)
                sc.wait_ge(S["yc"], 2 * it + 4)
                sc.dma_start(rows_q[bass.ds(it, 1), :, :].rearrange("o t n -> t (o n)"), ysb).then_inc(S["yo"], 16)

            with sc.Fori(0, last_it) as it:
                block_of(it, False)
            block_of(last_it, True)

        @block.vector
        def _(ve):
            chain = [0, S["chain"]]
            L = lambda ins: link(ve, chain, ins)
            tt, ts, stt, cp = ve.tensor_tensor, ve.tensor_scalar, ve.scalar_tensor_tensor, ve.tensor_copy
            M, A_, SUB = ALU.mult, ALU.add, ALU.subtract
            bc = lambda v, n, inner: v.unsqueeze(2).broadcast_to([P, n, inner])
            hv = lambda v: v.rearrange("p (h k) -> p h k", k=HD)

            ve.sem_inc(S["actd"], 2)
            ve.wait_ge(S["condq"], 1)
            cp(condf[:, 0, :], B[7][:, 0:16]).then_inc(S["condq"], 1)
            ve.wait_ge(S["condq"], 3)
            L(stt(condf[:, 1, :], condf[:, 1, :], 1.0, condf[:, 0, :], A_, M))
            ts(condT[:, :, :].rearrange("p k i -> p i k"), condf[:, 1, :].rearrange("p (i k) -> p i k", i=2),
               0.5, None, M).then_inc(S["condq"], 1)

            for j in range(NT):
                ve.wait_ge(s_xl[j], 16)
                L(ve.tensor_tensor_reduce(junk, xb[:, j, :], xb[:, j, :], 1.0, 0.0, M, A_, stat[:, j:j + 1]))
                ts(stat[:, 4 + j:5 + j], stat[:, j:j + 1], 1.0 / D, EPS, M, A_).then_inc(S["ssq"], 1)

            def modulation(m):
                if m == 0:
                    ve.wait_ge(S["bada"], 16)
                ve.wait_ge(S["wdone"], m + 1)
                seg = modrow[:, m * CH:(m + 1) * CH]
                tt(seg, ada_bank(m)[0:2, :], seg, A_).then_inc(S["modrow"], 1)

            for m in range(ADA1):
                modulation(m)
            ve.wait_ge(S["n1"], 16)
            ve.wait_ge(S["modb1"], 64)
            for i in range(2):
                L(stt(scb[:, i, :], scb[:, i, :], 1.0, nrm, A_, M))
            for j in range(NT):
                i = min(j, 1)
                ve.wait_ge(S["rstd"], j + 1)
                L(stt(xb[:, j, :], xb[:, j, :], stat[:, 8 + j:9 + j], scb[:, i, :], M, M))
                tt(xb[:, j, :], xb[:, j, :], shb[:, i, :], A_).then_inc(S["htok"], 1)
            ve.wait_ge(S["htok"], NT)
            for j in range(NT):
                for i in range(2):
                    ve.wait_ge(S["hTa"], 2 * j + i + 1)
                    seg = (slice(None), slice(4 * i, 4 * i + 4), slice(j * P, (j + 1) * P))
                    tt(hTp[1][seg], B[2 * (j % 2) + i].rearrange("p (k t) -> p k t", k=4), hTp[0][seg], SUB)\
                        .then_inc(S["hTv"], 1)
            for i in z_order(lambda t: z_low(ve, t)):
                m, j = zunits[i]
                if m < NZ and i % 2:
                    c, n = ZCHUNKS[m]
                    z_multiplied(ve, i)
                    cp(zbuf[:, j, c:c + n], B[i % 6][:, 0:n]).then_inc(S["zV"], 1)
            z_evacuated(ve, NZ * NT - 2)
            z_evacuated(ve, NZ * NT - 1)

            ve.wait_ge(S["mult"], ZQ_ALL)
            ve.wait_ge(S["cons2"], 16 * NCONS2)
            ve.wait_ge(S["cons3"], 16 * NCONS3)
            for j in range(NT):
                zq = zbuf[:, j, ZQ:ZQ + NQK * HD].rearrange("p (h k) -> p h k", k=HD)
                sqv = sq.rearrange("p (h k) -> p h k", k=HD)
                L(tt(sqv, zq, zq, M))
                L(ve.tensor_reduce(stat[:, 16:26], sqv, X, A_))
                ts(stat[:, 26:36], stat[:, 16:26], 1.0 / HD, EPS, M, A_).then_inc(S["anorm"], 1)
                ve.wait_ge(S["arstd"], j + 1)
                L(tt(qk[:, j, :, :], zq, bc(stat[:, 36:46], NQK, HD), M))
                L(tt(qk[:, j, 0:NHQ, :], qk[:, j, 0:NHQ, :], gqk[:, 0:1, :].broadcast_to([P, NHQ, HD]), M))
                ins = tt(qk[:, j, NHQ:NQK, :], qk[:, j, NHQ:NQK, :], gqk[:, 1:2, :].broadcast_to([P, NKV, HD]), M)
                if j == 0:
                    ins.then_inc(S["aqk"], 1)
                    continue
                L(ins)
                v5 = qk[:, j, :, :].rearrange("p h (a s i) -> p h a s i", a=2, s=2)
                x1_, x2_ = v5[:, :, :, 0, :], v5[:, :, :, 1, :]
                cs = [rope[:, j - 1:j, t, :, :].broadcast_to([P, NQK, 2, 16]) for t in range(2)]
                r4 = [rt[:, t, :].rearrange("p (h a i) -> p h a i", h=NQK, a=2) for t in range(4)]
                L(tt(r4[0], x1_, cs[0], M))
                L(tt(r4[1], x2_, cs[1], M))
                L(tt(r4[2], x2_, cs[0], M))
                L(tt(r4[3], x1_, cs[1], M))
                L(tt(x1_, r4[0], r4[1], SUB))
                tt(x2_, r4[2], r4[3], A_).then_inc(S["aqk"], 1)
            for m in range(ADA1, ADA2):
                modulation(m)
            ve.wait_ge(S["cachekv"], 32)
            for j in range(NT + 1):
                src = qk[:, j, NHQ:NQK, :] if j < NT else ckv[:, 0, :].rearrange("p (g k) -> p g k", g=NKV)
                ve.wait_ge(S["aqk"], min(j + 1, NT))
                for g in range(NKV):
                    ins = cp(kdup[:, 2 * g:2 * g + 2, :], src[:, g:g + 1, :].broadcast_to([P, 2, HD]))
                ins.then_inc(S["kdupd"], 1)
                ve.wait_ge(S["ktr"], j + 1)
                cp(KT[:, :, j * P:(j + 1) * P], B[1][:, 0:2 * P].rearrange("p (g t) -> p g t", g=NKV))\
                    .then_inc(S["kTv"], 1)

            def row_max(n):
                nk = P if aunits[n][0] == 0 else 3 * P
                ve.wait_ge(S["smm"], n + 1)
                if n >= 2:
                    ve.wait_ge(S["prob"], n - 1)
                L(ve.tensor_reduce(stat[:, 48 + n % 2:49 + n % 2], B[2 + n % 2][:, 0:nk], X, ALU.max))
                ts(stat[:, 50 + n % 2:51 + n % 2], stat[:, 48 + n % 2:49 + n % 2], -SCALE, None, M).then_inc(S["nmax"], 1)

            def probs_back(n):
                nk = P if aunits[n][0] == 0 else 3 * P
                ve.wait_ge(S["prob"], n + 1)
                if n >= 2:
                    ve.wait_ge(S["ya"], n - 1)
                ve.reciprocal(stat[:, 54 + n % 2:55 + n % 2], stat[:, 52 + n % 2:53 + n % 2]).then_inc(S["rinv"], 1)
                ve.wait_ge(S["ptr"], n + 1)
                cp(probT[:, n % 2, 0:nk], B[4 + n % 2][:, 0:nk]).then_inc(S["ptc"], 1)

            for n in range(len(aunits) + 1):
                if n < len(aunits):
                    row_max(n)
                if n >= 1:
                    probs_back(n - 1)
                m = ADA2 + n // 4 - 1
                if n % 4 == 0 and ADA2 <= m < ADA:
                    modulation(m)

            ve.wait_ge(S["tg"], 2)
            ts(zbuf[:, :, ZGD:ZGD + P], zbuf[:, :, ZGD:ZGD + P], 0.5, 0.5, M, A_).then_inc(S["sgd"], 1)
            ve.wait_ge(S["zfill"], 16 * NEXTRA)
            for j in range(NT):
                kj = kkn[:, j, :]
                L(tt(kj, zbuf[:, j, ZK:ZK + DR], kkb, M))
                L(tt(sq[:, 0:DR], kj, kj, M))
                L(ve.tensor_reduce(stat[:, 0:8], hv(sq[:, 0:DR]), X, A_))
                ts(stat[:, 8:16], stat[:, 0:8], KK_EPS, None, A_).then_inc(S["kkss"], 1)
                ve.wait_ge(S["kkr"], j + 1)
                tt(hv(kj), hv(kj), bc(stat[:, 16:24], HR, HD), M).then_inc(S["kkd"], 1)
            ve.wait_ge(S["ttr"], 2)
            cp(adT, B[1][:, 0:NT * P]).then_inc(S["tcV"], 1)
            for d in range(2):
                ve.wait_ge(S["sttr"], d + 1)
                cp(states[:, d, :, :], B[3][:, 0:4 * HD].rearrange("p (c v) -> p c v", c=4)).then_inc(S["stev"], 1)

            ve.wait_ge(S["modd"], 32)
            L(ve.memset(S0P, 0.0))
            touched = set()
            for u, (d, j) in enumerate(units):
                lat = j > 0
                zr, zk = zbuf[:, j, ZR:ZR + DR], zbuf[:, j, ZK:ZK + DR]
                for i, (t, row) in enumerate(((T1, w0b), (T2, a0b))):
                    ve.wait_ge(S["lora"], 2 * u + i + 1)
                    tt(t, B[i], row[:, d, :], A_).then_inc(S["lt1"], 1)
                ve.wait_ge(S["ltanh"], 2 * u + 1)
                ts(LW, T1, -CDEC / 2, -CDEC / 2, M, A_).then_inc(S["lw"], 1)
                ve.wait_ge(S["ltanh"], 2 * u + 2)
                L(ts(AA, T2, 0.5, 0.5, M, A_))
                L(stt(T1, AA, -1.0, kab, A_, M))
                L(stt(KD, T1, 1.0, zk, A_, M))
                L(tt(T2, kkn[:, j, :], AA, M))
                ve.wait_ge(S["lexp"], 4 * u + 2)
                tt(BT_, T2, EN, M).then_inc(S["bkd"], 1)
                tt(KT_, KD, EN, M).then_inc(S["bkd"], 1)
                L(tt(T1, KD, zr, M))
                L(tt(T1, T1, rkb, M))
                L(ve.tensor_reduce(bonus[:, j, d, :], hv(T1), X, A_))
                if lat:
                    ve.wait_ge(S["lexp"], 4 * u + 4)
                    for i in range(2):
                        r = slice(i * HD, (i + 1) * HD)
                        ins = tt(S0P[r, :, i, :], states[r, d, :, :], ecol[r, :, 0:1].broadcast_to([HD, 4, HD]), M)
                        L(ins) if i == 0 else ins.then_inc(S["s0p"], 1)
                for i, dst in enumerate((BTT, KTT)):
                    ve.wait_ge(S["ttr4"], 4 * u + 3 + i)
                    cp(dst.rearrange("p a b -> p (a b)"), B[5 + i]).then_inc(S["bkT"], 1)
                for h in range(HR):
                    ve.wait_ge(S["gram"], 8 * u + h + 1)
                    tt(AM[:, h, :, :].rearrange("p a b -> p (a b)"), B[gbank[h]], gramm[:, d, :], M).then_inc(S["am"], 1)
                idb = ident[:, :].unsqueeze(1).broadcast_to([P, 4, P])
                b4 = lambda b: B[b].rearrange("p (a b) -> p a b", a=4)
                for g in range(2):
                    ve.wait_ge(s_at[g], 7 * u + 1)
                    ve.wait_ge(s_p[g], 6 * u + 1)
                    tt(XM[g], idb, b4(2 + 3 * g), SUB).then_inc(S["chain"], 1)
                    chain[0] += 1
                    tt(XT[g], idb, ATL[g][0], SUB).then_inc(s_x[g], 1)
                for l in range(1, LEVELS - 1):
                    for g in range(2):
                        ve.wait_ge(s_d[g], 5 * u + l)
                        ve.wait_ge(s_x[g], 6 * u + l)
                        if l < LEVELS - 2:
                            tt(XM[g], XM[g], b4(3 + 3 * g), SUB).then_inc(S["chain"], 1)
                            chain[0] += 1
                        tt(XT[g], XT[g], b4(4 + 3 * g), SUB).then_inc(s_x[g], 1)
                for g in range(2):
                    ve.wait_ge(s_u[g], 4 * u + 4)
                    ve.wait_ge(s_uc[g], 4 * u + 3)
                    tt(UU[g].rearrange("p a b -> p (a b)"), B[2 + 3 * g][:, 0:4 * HD],
                       U1[g].rearrange("p a b -> p (a b)"), SUB).then_inc(s_uc[g], 1)
                for g in range(2):
                    ve.wait_ge(S["yout"], 2 * u + g + 1)
                    dst = yrw[:, j, g * 256:(g + 1) * 256]
                    if (j, g) in touched:
                        ve.wait_ge(S["yrd"], 2 * u + g)
                        tt(dst, B[3 + 3 * g][:, 0:256], dst, A_).then_inc(S["yrd"], 1)
                    else:
                        cp(dst, B[3 + 3 * g][:, 0:256]).then_inc(S["yrd"], 1)
                    touched.add((j, g))
                    if u in LAST:
                        continue
                    ve.wait_ge(S["twod"], st_index[u] + g + 1)
                    t2 = B[4 + 3 * g][:, 0:2 * HD].rearrange("p (c v) -> p c v", c=2)
                    end = ecol[:, 2 * g:2 * g + 2, 1:2].broadcast_to([P, 2, HD])
                    if lat:
                        s = states[:, d, 2 * g:2 * g + 2, :]
                        for i in range(2):
                            r = slice(i * HD, (i + 1) * HD)
                            L(tt(s[r], t2[r], S0P[r, 2 * g:2 * g + 2, i, :], A_))
                        tt(s, s, end, M).then_inc(S["st2"], 1)
                    else:
                        ve.wait_ge(S["lexp"], 4 * u + 4)
                        tt(sfin[:, 2 * g:2 * g + 2, :], t2, end, M).then_inc(S["st2"], 1)
                if u not in LAST:
                    ve.wait_ge(S["st2"], st_index[u] + 2)

            ve.wait_ge(S["yrd"], 2 * NU)
            ve.wait_ge(S["lnld"], 32)
            for j in range(NT):
                L(ve.tensor_reduce(stat[:, 0:8], hv(yrw[:, j, :]), X, A_))
                L(ts(stat[:, 0:8], stat[:, 0:8], 1.0 / HD, None, M))
                if j:
                    ve.wait_ge(S["ytr"], 2 * j - 1)
                L(tt(hv(yc), hv(yrw[:, j, :]), bc(stat[:, 0:8], HR, HD), SUB))
                L(tt(ysq, yc, yc, M))
                L(ve.tensor_reduce(stat[:, 24:32], hv(ysq), X, A_))
                ts(stat[:, 8:16], stat[:, 24:32], 1.0 / HD, GN_EPS, M, A_).then_inc(S["kkss"], 1)
                ve.wait_ge(S["kkr"], NT + j + 1)
                L(tt(hv(yc), hv(yc), bc(stat[:, 16:24], HR, HD), M))
                L(tt(yc, yc, lnw, M))
                L(tt(yc, yc, lnb, A_))
                L(tt(stat[:, 24:32], bonus[:, j, 0, :], bonus[:, j, 1, :], A_))
                L(tt(hv(ysq), hv(zbuf[:, j, ZV:ZV + DR]), bc(stat[:, 24:32], HR, HD), M))
                L(tt(yc, yc, ysq, A_))
                ve.wait_ge(S["gps"], j + 1)
                tt(yc, B[6], yc, M).then_inc(S["yfin"], 1)
                ve.wait_ge(S["upm"], j + 1)
                ve.wait_ge(S["gld"], 16 * (j + 1))
                if j:
                    ve.wait_ge(S["mtr"], 2 * j)
                for i, dst in enumerate((mg, mg2)):
                    for n in range(2):
                        L(stt(dst[:, n * CH:(n + 1) * CH], gld[:, i * D + n * CH:i * D + (n + 1) * CH], 1.0,
                              B[2 * i + n], A_, M))
                tt(mg, mg, mg2, A_).then_inc(S["mrg"], 1)
            for j in range(NT):
                ve.wait_ge(s_xl[j], 32)
                ve.wait_ge(S["g1l"], 16 * (1 + min(j, 1)))
                for n in range(2):
                    ve.wait_ge(S["wout"], 2 * j + n + 1)
                    seg = slice(n * CH, (n + 1) * CH)
                    L(tt(x1[:, j, seg], B[2 * (j % 2) + n], g1b[:, seg], M))
                    ins = tt(x1[:, j, seg], x1[:, j, seg], xr2[:, seg], A_)
                    if n == 0:
                        L(ins)
                    else:
                        ins.then_inc(S["x1s"], 1)
            ve.wait_ge(S["x1s"], NT)
            for j in range(NT):
                L(ve.tensor_tensor_reduce(jk, x1[:, j, :], x1[:, j, :], 1.0, 0.0, M, A_, stat[:, j:j + 1]))
                ts(stat[:, 4 + j:5 + j], stat[:, j:j + 1], 1.0 / D, EPS, M, A_).then_inc(S["ssq"], 1)
            ve.wait_ge(S["n1"], 32)
            for j in range(NT):
                if j < 2:
                    ve.wait_ge(S["n2l"], 32 * (j + 1))
                    L(stt(sc2, sc2, 1.0, n2, A_, M))
                ve.wait_ge(S["rstd"], NT + j + 1)
                if j:
                    ve.wait_ge(S["h2out"], 16 * j)
                    ve.wait_ge(S["h2tr"], 2 * j)
                L(stt(h2, x1[:, j, :], stat[:, 8 + j:9 + j], sc2, M, M))
                tt(h2, h2, sh2, A_).then_inc(S["h2s"], 1)

            ve.wait_ge(S["lg"], NT)
            ve.wait_ge(S["cons3"], 16 * (NCONS3 + NCONS4))
            lv = lgt[:, :, :]
            L(tt(lv, B[6][:, 0:NT * NE].rearrange("p (j e) -> p j e", j=NT),
                 brow.unsqueeze(1).broadcast_to([P, NT, NE]), A_))
            for j in range(NT):
                L(ve.max(mx8[:, j, :], lgt[:, j, :]))
                L(ve.max_index(ix8[:, j, :], mx8[:, j, :], lgt[:, j, :]))
            tt(exd, mx8[:, :, 0:TOPK], mx8[:, :, 0:1].broadcast_to([P, NT, TOPK]), SUB).then_inc(S["exa"], 1)
            L(cp(ixf.rearrange("p (j k) -> p j k", j=NT), ix8[:, :, 0:TOPK]))
            L(tt(onehot, iota[:, 0:NE].unsqueeze(1).broadcast_to([P, 12, NE]),
                 ixf.unsqueeze(2).broadcast_to([P, 12, NE]), ALU.is_equal))
            for j in range(NT):
                ins = ve.tensor_reduce(selm[:, j, :], onehot[:, 4 * j:4 * j + 4, :].rearrange("p k e -> p e k"), X, A_)
                L(ins) if j < NT - 1 else ins.then_inc(S["routeq"], 1)
            ve.wait_ge(S["exb"], 1)
            L(ve.tensor_reduce(sum3, exd, X, A_))
            L(ve.reciprocal(sum3, sum3))
            L(tt(gate[:, :, :], exd, sum3.unsqueeze(2).broadcast_to([P, NT, TOPK]), M))
            ve.wait_ge(S["routeq"], 3)
            L(cp(rkm, B[7][:, 0:NT * NE].rearrange("p (j e) -> p j e", j=NT)))
            L(tt(acol, B[5][0:QMAX, 0:1], cq[0:QMAX, 2:3], ALU.is_gt))
            cp(aspread, acol.broadcast_to([QMAX, P])).then_inc(S["routeq"], 1)
            ve.wait_ge(S["routeq"], 1)
            L(stt(rsel, rkm, 1000.0, selm, A_, M))
            for q in range(NB):
                L(ts(rankm[:, :, q * NE:(q + 1) * NE], rsel, -1000.0 - P * q, None, A_))
            ve.wait_ge(S["routeq"], 5)
            L(cp(pcol, B[4][0:QMAX, 0:1]))
            L(cp(posb, B[4][:, P:P + QMAX]))
            ts(lsto, iota[0:QMAX, :], pcol, acol, ALU.is_equal, M).then_inc(S["routeq"], 1)
            for j in range(NT):
                ins = ts(cmp[:, j, :], iota, rankm[:, j, 0:1], None, ALU.is_equal)
            ins.then_inc(S["cmpd"], 1)
            ve.wait_ge(S["routeq"], 7)
            L(ts(tab[:, 2 * P + 1:], B[3][0:1, 2 * P:2 * P + 1], -1.0, None, A_))
            cp(tab[:, 0:2 * P + 1], B[3][0:1, 0:2 * P + 1]).then_inc(S["routeq"], 1)
            for j in range(NT):
                L(tt(ohr[:, 4 * j:4 * j + 4, :], onehot[:, 4 * j:4 * j + 4, :],
                     rkm[:, j:j + 1, :].broadcast_to([P, 4, NE]), M))
            L(ve.tensor_reduce(rkf, ohr, X, A_))
            L(tt(pdif, posb[:, NE:QMAX], posb[:, 0:QMAX - NE], SUB))
            for i in range(2):
                L(tt(ohr, onehot, pdif[:, i * NE:(i + 1) * NE].unsqueeze(1).broadcast_to([P, 12, NE]), M))
                L(ve.tensor_reduce(d12[i], ohr, X, A_))
                L(ts(d12[i], d12[i], -1.0, float(P), A_, M))
            L(stt(ixf, ixf, float(P), rkf, M, A_))
            for i in range(2):
                L(stt(s12, rkf, float(P * (i + 1)), d12[i], ALU.is_ge, M))
                ins = tt(ixf if i == 0 else dest[:, :], ixf, s12, A_)
                L(ins)
            def rows_turned(h, count):
                ve.wait_ge(S["xtc"], count)
                tt(xTp[1][:, 4 * h:4 * h + 4, :], B[7].rearrange("p (k t) -> p k t", k=4),
                   xTp[0][:, 4 * h:4 * h + 4, :], SUB).then_inc(S["xtl"], 1)

            rows_turned(0, 1)
            rows_turned(1, 2)
            last_it = ve.value_load(tab[0:1, 2 * P + 1:2 * P + 2], min_val=NE - 1, max_val=NBMAX - 1)

            def block_of(it, last):
                lchain = [0, S["chain2v"]]
                PER = 4
                LL = lambda ins: link(ve, lchain, ins, PER * it)

                def clamp_gate(h):
                    ve.wait_ge(S["mult"], WC * it + (4 * h + 2 + ZQ_ALL))
                    ts(gl, B[2 * h], LIMIT, None, ALU.min).then_inc(S["gld2"], 1)

                def activate(h):
                    ve.wait_ge(S["mult"], WC * it + (4 * h + 4 + ZQ_ALL))
                    ve.wait_ge(S["actd"], 2 * it + (h + 2))
                    LL(ts(uu, B[2 * h + 1], LIMIT, -LIMIT, ALU.min, ALU.max))
                    ve.wait_ge(S["gld2"], 2 * it + (h + 1))
                    LL(stt(uu, uu, 1.0, gl, A_, M))
                    ve.wait_ge(S["thd"], 2 * it + (h + 1))
                    stt(act[:, h * CH:(h + 1) * CH], th, 1.0, uu, A_, M).then_inc(S["actd"], 1)

                def act_turned(h):
                    ve.wait_ge(S["atc"], 2 * it + (h + 1))
                    stt(actTp[1][:, 4 * h:4 * h + 4, :], B[6].rearrange("p (k t) -> p k t", k=4), 0.5,
                        actTp[0][:, 4 * h:4 * h + 4, :], M, SUB).then_inc(S["atl"], 1)

                for c in range(NPAIR, WC if last else WC + NPAIR):
                    if c == 7:
                        activate(0)
                    if c == 10:
                        activate(1)
                        if not last:
                            rows_turned(0, 2 * it + 3)
                    if c == 11:
                        act_turned(1)
                        if not last:
                            rows_turned(1, 2 * it + 4)
                    if c % WC not in POOL_LO:
                        low_part(ve, it, c)
                    if c == NPAIR and not last:
                        q = ve.value_load(tab[0:1, bass.ds(it + 1, 1)], min_val=0, max_val=QMAX - 1)
                        ve.wait_ge(S["idxm"], it + 1)
                        for j in range(NT):
                            ins = ts(cmp[:, j, :], iota, rankm[:, j, bass.ds(q, 1)], None, ALU.is_equal)
                        ins.then_inc(S["cmpd"], 1)
                    if c == 5:
                        clamp_gate(0)
                    if c == 9:
                        act_turned(0)
                        clamp_gate(1)
                assert lchain[0] == PER
                ve.wait_ge(S["ymm"], it + 1)
                ve.wait_ge(S["yo"], 16 * it + 16)
                cp(ysb[:, 0:CH], B[4]).then_inc(S["yc"], 1)

            with ve.Fori(0, last_it) as it:
                block_of(it, False)
            block_of(last_it, True)

            ve.wait_ge(S["fld"], 48)
            for j in range(NT):
                ve.wait_ge(s_yg[j], 16 * TOPK)
                if j:
                    ve.wait_ge(S["fin"], j)
                L(ts(facc, ygat[TOPK * j], gate[:, j, 0:1], None, M))
                for k in range(1, TOPK):
                    L(stt(facc, ygat[TOPK * j + k], gate[:, j, k:k + 1], facc, M, A_))
                L(tt(facc, facc, g2b[min(j, 1)], M))
                L(tt(facc, facc, x1[:, j, :], A_))
                L(ve.tensor_tensor_reduce(jk, facc, facc, 1.0, 0.0, M, A_, stat[:, j:j + 1]))
                ts(stat[:, 4 + j:5 + j], stat[:, j:j + 1], 1.0 / D, EPS, M, A_).then_inc(S["ssq"], 1)
                ve.wait_ge(S["rstd"], 2 * NT + j + 1)
                stt(x1[:, j, :], facc, stat[:, 8 + j:9 + j], nfb, M, M).then_inc(S["fin"], 1)


_INS = ["x_prompt", "x_sample", "cache_k", "cache_v", "state_rwkv_fwd", "state_rwkv_bwd", "c", "c_ctx", "w_ada",
        "b_ada", "norm1", "norm2", "w_in", "rw_w0", "rw_w2", "rw_a0", "rw_a2", "rw_g2", "rw_kk", "rw_ka", "rw_rk",
        "rw_ln_w", "rw_ln_b", "q_norm", "k_norm", "w_up_r", "w_up_a", "w_out", "w_router", "b_router",
        "w_moe_in", "b_moe_in", "w_moe_out", "b_moe_out", "norm_f"]
_OUTS = [("y_prompt", (1, P, D)), ("y_sample", (1, 2 * P, D)), ("new_cache_k", (1, 1, P, NKV, HD)),
         ("new_cache_v", (1, 1, P, NKV, HD)), ("new_state_fwd", (1, 1, HR, HD, HD)),
         ("new_state_bwd", (1, 1, HR, HD, HD))]


def kernel(**inputs):
    import concourse.bacc as bacc
    from concourse.bass_utils import run_bass_kernel_spmd

    nc = bacc.Bacc("TRN2", target_bir_lowering=False, num_devices=1, dynamic_dma_scratch_size=8192)
    arrays, a, o = {}, {}, {}
    for name in _INS:
        arrays[name] = np.ascontiguousarray(inputs[name])
    arrays.update(_CONST)
    for name, v in arrays.items():
        a[name] = nc.dram_tensor(name, v.shape, mybir.dt.from_np(v.dtype), kind="ExternalInput").ap()
    for name, shape in _OUTS:
        o[name] = nc.dram_tensor(name, shape, F32, kind="ExternalOutput").ap()
    build(nc, a, o)
    r = run_bass_kernel_spmd(nc, [arrays], core_ids=[0])
    return tuple(r.results[0][name] for name, _ in _OUTS)
```
